# Optimizing a Trainium2 kernel written in Bass

```python
import math
import jax, jax.numpy as jnp
from jax import lax
import numpy as np
import jax
import jax.numpy as jnp

D_MODEL = 1024
BATCH = 1
SEQ = 256
DEPTH = 2

N_MIXERS = 2
N_CONV_LAYERS = (DEPTH + 1) // 2
N_ATTN_LAYERS = DEPTH // 2
D_FF = 2816
CONV_WIDTH = 31
N_HEADS = 16
HEAD_DIM = D_MODEL // N_HEADS
D_ATTN = N_HEADS * HEAD_DIM
BLOCK_Q = 128
RMS_EPS = 1e-6
LN_EPS = 1e-5


def rms_norm(x, g):
    xf = x.astype(jnp.float32)
    y = xf * lax.rsqrt(jnp.mean(xf * xf, axis=-1, keepdims=True) + RMS_EPS)
    return (y * g.astype(jnp.float32)).astype(x.dtype)

def layer_norm(x, g, b):
    xf = x.astype(jnp.float32)
    mu = jnp.mean(xf, axis=-1, keepdims=True)
    var = jnp.mean(jnp.square(xf - mu), axis=-1, keepdims=True)
    y = (xf - mu) * lax.rsqrt(var + LN_EPS)
    return (y * g.astype(jnp.float32) + b.astype(jnp.float32)).astype(x.dtype)

def swiglu_ffn(h, w_in, w_out):
    gate, up = jnp.split(h @ w_in, 2, axis=-1)
    return (jax.nn.silu(gate) * up) @ w_out

def conformer_conv(h, w_pw1, b_pw1, w_dw, b_dw, ln_g, ln_b, w_pw2, b_pw2):
    val, gate = jnp.split(h @ w_pw1 + b_pw1, 2, axis=-1)
    u = val * jax.nn.sigmoid(gate)
    u = lax.conv_general_dilated(
        u, w_dw[:, None, :].astype(u.dtype),
        window_strides=(1,),
        padding=((CONV_WIDTH - 1, 0),),
        dimension_numbers=("NWC", "WIO", "NWC"),
        feature_group_count=D_MODEL,
    ) + b_dw
    u = jax.nn.silu(layer_norm(u, ln_g, ln_b))
    return u @ w_pw2 + b_pw2

def stick_breaking_attention(h, w_qkv, w_o):
    b, s, _ = h.shape
    qkv = (h @ w_qkv).reshape(b, s, 3, N_HEADS, HEAD_DIM)
    qkv = jnp.transpose(qkv, (2, 0, 3, 1, 4))
    q, k, v = qkv[0], qkv[1], qkv[2]
    n_blk = s // BLOCK_Q
    q_blocks = jnp.transpose(q.reshape(b, N_HEADS, n_blk, BLOCK_Q, HEAD_DIM), (2, 0, 1, 3, 4))
    starts = jnp.arange(n_blk, dtype=jnp.int32) * BLOCK_Q
    key_pos = jnp.arange(s, dtype=jnp.int32)
    scale = 1.0 / math.sqrt(HEAD_DIM)

    def one_block(args):
        qb, start = args
        z = jnp.einsum("bhqd,bhkd->bhqk", qb, k).astype(jnp.float32) * scale
        q_pos = start + jnp.arange(BLOCK_Q, dtype=jnp.int32)
        mask = key_pos[None, :] < q_pos[:, None]
        log_beta = jax.nn.log_sigmoid(z)
        log_1m = jnp.where(mask, log_beta - z, 0.0)
        suffix = lax.cumsum(log_1m, axis=3, reverse=True) - log_1m
        a = jnp.where(mask, jnp.exp(log_beta + suffix), 0.0)
        return jnp.einsum("bhqk,bhkd->bhqd", a.astype(v.dtype), v)

    out = lax.map(one_block, (q_blocks, starts))
    out = jnp.transpose(out, (1, 0, 3, 2, 4)).reshape(b, s, D_ATTN)
    return out @ w_o

def first_inputs(seed: int = 0) -> dict:
    key = jax.random.key(seed)
    ks = jax.random.split(key, 16)
    f32 = jnp.float32
    nrm = lambda k, shape, scale: jax.random.normal(k, shape, f32) * scale
    return {
        "x": jax.random.normal(ks[0], (BATCH, SEQ, D_MODEL), f32),
        "norm_g": 1.0 + nrm(ks[1], (DEPTH, 3, D_MODEL), 0.01),
        "final_g": 1.0 + nrm(ks[2], (D_MODEL,), 0.01),
        "ffn_w_in": nrm(ks[3], (DEPTH, 2, D_MODEL, 2 * D_FF), D_MODEL ** -0.5),
        "ffn_w_out": nrm(ks[4], (DEPTH, 2, D_FF, D_MODEL), D_FF ** -0.5),
        "conv_w_pw1": nrm(ks[5], (N_CONV_LAYERS, D_MODEL, 2 * D_MODEL), D_MODEL ** -0.5),
        "conv_b_pw1": nrm(ks[6], (N_CONV_LAYERS, 2 * D_MODEL), 0.01),
        "conv_w_dw": nrm(ks[7], (N_CONV_LAYERS, CONV_WIDTH, D_MODEL), CONV_WIDTH ** -0.5),
        "conv_b_dw": nrm(ks[8], (N_CONV_LAYERS, D_MODEL), 0.01),
        "conv_ln_g": 1.0 + nrm(ks[9], (N_CONV_LAYERS, D_MODEL), 0.01),
        "conv_ln_b": nrm(ks[10], (N_CONV_LAYERS, D_MODEL), 0.01),
        "conv_w_pw2": nrm(ks[11], (N_CONV_LAYERS, D_MODEL, D_MODEL), D_MODEL ** -0.5),
        "conv_b_pw2": nrm(ks[12], (N_CONV_LAYERS, D_MODEL), 0.01),
        "attn_w_qkv": nrm(ks[13], (N_ATTN_LAYERS, D_MODEL, 3 * D_ATTN), D_MODEL ** -0.5),
        "attn_w_o": nrm(ks[14], (N_ATTN_LAYERS, D_ATTN, D_MODEL), D_ATTN ** -0.5),
    }

def first_block(x, norm_g, final_g, ffn_w_in, ffn_w_out,
              conv_w_pw1, conv_b_pw1, conv_w_dw, conv_b_dw, conv_ln_g, conv_ln_b,
              conv_w_pw2, conv_b_pw2, attn_w_qkv, attn_w_o):
    for i in range(DEPTH):
        g = norm_g[i]
        x = x + 0.5 * swiglu_ffn(rms_norm(x, g[0]), ffn_w_in[i, 0], ffn_w_out[i, 0])
        h = rms_norm(x, g[1])
        j = i // N_MIXERS
        if i % N_MIXERS == 0:
            x = x + conformer_conv(h, conv_w_pw1[j], conv_b_pw1[j], conv_w_dw[j], conv_b_dw[j],
                                   conv_ln_g[j], conv_ln_b[j], conv_w_pw2[j], conv_b_pw2[j])
        else:
            x = x + stick_breaking_attention(h, attn_w_qkv[j], attn_w_o[j])
        x = x + 0.5 * swiglu_ffn(rms_norm(x, g[2]), ffn_w_in[i, 1], ffn_w_out[i, 1])
    return rms_norm(x, final_g)


_first_inputs = first_inputs


def first_inputs(seed=0):
    import zlib

    import numpy as np

    out = dict(_first_inputs(seed))
    spreads = {}
    factors = {'norm_g': 4.982,
     'final_g': 31.096,
     'conv_b_pw1': 8.0,
     'conv_b_dw': 14.248,
     'conv_ln_g': 38.644,
     'conv_ln_b': 40.73,
     'conv_b_pw2': 28.108}
    for name, (base, spread) in spreads.items():
        noise = np.random.default_rng([zlib.crc32(name.encode()), seed]).standard_normal(out[name].shape)
        drawn = base * np.exp(spread * noise) if base else spread * noise
        out[name] = __import__('jax').numpy.asarray(drawn.astype(out[name].dtype))
    for name, factor in factors.items():
        out[name] = (out[name] * factor).astype(out[name].dtype)
    return out


_narrow_inputs = first_inputs


def first_inputs(seed=0):

    out = dict(_narrow_inputs(seed))
    wider = {'final_g': 6.31, 'conv_ln_g': 5.26, 'conv_ln_b': 5.12, 'conv_b_pw2': 5.22}
    for name, times in wider.items():
        mean = out[name].mean()
        out[name] = (mean + times * (out[name] - mean)).astype(out[name].dtype)
    return out


DEPTH_2 = 1

MLA_HEADS = 8
MLA_NOPE = 128
MLA_ROPE = 64
MLA_V = 128
Q_LORA = 384
KV_LORA = 256
MOBA_HEADS = 8
MOBA_HD = 128
MOBA_BLOCK = 256
MOBA_TOPK = 3
MOBA_QCHUNK = 32
Q_BLOCK = 128
CONV_W = 3

ROPE_THETA = 10000.0
EPS = 1e-6
NEG = -1e30
N_BRANCH = 2

OFF_QLAT = 0
OFF_KVLAT = OFF_QLAT + Q_LORA
OFF_KPE = OFF_KVLAT + KV_LORA
OFF_MOBA = OFF_KPE + MLA_ROPE
OFF_GATE = OFF_MOBA + 3 * MOBA_HEADS * MOBA_HD
IN_COLS = OFF_GATE + N_BRANCH * D_MODEL


F32 = jnp.float32

def rmsnorm(x, g):
    xf = x.astype(F32)
    y = xf * lax.rsqrt(jnp.mean(xf * xf, axis=-1, keepdims=True) + EPS)
    return (y * g.astype(F32)).astype(x.dtype)

def rope(x, pos):
    d = x.shape[-1]
    inv = ROPE_THETA ** (-jnp.arange(0, d, 2, dtype=F32) / d)
    ang = pos.astype(F32)[:, None] * inv[None, :]
    cos, sin = jnp.cos(ang), jnp.sin(ang)
    x1, x2 = jnp.split(x.astype(F32), 2, axis=-1)
    out = jnp.concatenate([x1 * cos - x2 * sin, x1 * sin + x2 * cos], axis=-1)
    return out.astype(x.dtype)

def causal_attention_blocks(q, k, v, scale):
    B, H, S, Dk = q.shape
    nq = S // Q_BLOCK
    qb = jnp.moveaxis(q.reshape(B, H, nq, Q_BLOCK, Dk), 2, 0)
    kpos = jnp.arange(S)

    def blk_fn(args):
        i, qi = args
        qpos = i * Q_BLOCK + jnp.arange(Q_BLOCK)
        s = jnp.einsum('bhqd,bhkd->bhqk', qi, k).astype(F32) * scale
        s = jnp.where(kpos[None, :] <= qpos[:, None], s, NEG)
        p = jax.nn.softmax(s, axis=-1).astype(v.dtype)
        return jnp.einsum('bhqk,bhkd->bhqd', p, v)

    out = lax.map(blk_fn, (jnp.arange(nq), qb))
    return jnp.moveaxis(out, 0, 2).reshape(B, H, S, v.shape[-1])

def moba_attention(q, k, v):
    B, H, S, D = q.shape
    nb = -(-S // MOBA_BLOCK)
    Sp = nb * MOBA_BLOCK
    pad = ((0, 0), (0, 0), (0, Sp - S), (0, 0))
    q, k, v = jnp.pad(q, pad), jnp.pad(k, pad), jnp.pad(v, pad)
    kb = k.reshape(B, H, nb, MOBA_BLOCK, D)
    vb = v.reshape(B, H, nb, MOBA_BLOCK, D)
    kmean = jnp.mean(kb.astype(F32), axis=3)
    gate = jnp.einsum('bhsd,bhnd->bhsn', q.astype(F32), kmean)
    q_blk = jnp.arange(Sp) // MOBA_BLOCK
    past = jnp.arange(nb)[None, :] < q_blk[:, None]
    gate = jnp.where(past, gate, -jnp.inf)
    k_sel = min(MOBA_TOPK, nb)
    top_s, top_idx = lax.top_k(gate, k_sel)
    top_ok = jnp.isfinite(top_s)

    nc = Sp // MOBA_QCHUNK

    def to_chunks(t):
        return jnp.moveaxis(t.reshape((B, H, nc, MOBA_QCHUNK) + t.shape[3:]), 2, 0)

    scale = D ** -0.5
    gather = jax.vmap(jax.vmap(lambda t, ix: t[ix]))

    def chunk_fn(args):
        c, qc, ic, okc = args
        qpos = c * MOBA_QCHUNK + jnp.arange(MOBA_QCHUNK)
        blk = (c * MOBA_QCHUNK) // MOBA_BLOCK
        ks = gather(kb, ic)
        vs = gather(vb, ic)
        ko = lax.dynamic_index_in_dim(kb, blk, axis=2, keepdims=False)
        vo = lax.dynamic_index_in_dim(vb, blk, axis=2, keepdims=False)
        s_sel = jnp.einsum('bhcd,bhckjd->bhckj', qc, ks).astype(F32) * scale
        s_sel = jnp.where(okc[..., None], s_sel, NEG)
        s_own = jnp.einsum('bhcd,bhjd->bhcj', qc, ko).astype(F32) * scale
        kpos = blk * MOBA_BLOCK + jnp.arange(MOBA_BLOCK)
        s_own = jnp.where(kpos[None, :] <= qpos[:, None], s_own, NEG)
        s = jnp.concatenate([s_sel.reshape(B, H, MOBA_QCHUNK, k_sel * MOBA_BLOCK), s_own], axis=-1)
        p = jax.nn.softmax(s, axis=-1).astype(v.dtype)
        p_sel = p[..., :k_sel * MOBA_BLOCK].reshape(B, H, MOBA_QCHUNK, k_sel, MOBA_BLOCK)
        p_own = p[..., k_sel * MOBA_BLOCK:]
        return (jnp.einsum('bhckj,bhckjd->bhcd', p_sel, vs)
                + jnp.einsum('bhcj,bhjd->bhcd', p_own, vo))

    out = lax.map(chunk_fn, (jnp.arange(nc), to_chunks(q), to_chunks(top_idx), to_chunks(top_ok)))
    return jnp.moveaxis(out, 0, 2).reshape(B, H, Sp, D)[:, :, :S]

def causal_dwconv(u, w, b):
    S = u.shape[1]
    up = jnp.pad(u, ((0, 0), (CONV_W - 1, 0), (0, 0)))
    y = b
    for j in range(CONV_W):
        y = y + w[j] * up[:, j:j + S]
    return y

def second_inputs(seed: int = 0) -> dict:
    key = jax.random.key(seed)
    ks = jax.random.split(key, 20)
    L = DEPTH_2

    def w(k, shape, fan_in):
        return jax.random.normal(k, shape, F32) * fan_in ** -0.5

    def gain(k, shape):
        return 1.0 + 0.02 * jax.random.normal(k, shape, F32)

    return {
        'x': jax.random.normal(ks[0], (BATCH, SEQ, D_MODEL), F32),
        'attn_norm': gain(ks[1], (L, D_MODEL)),
        'w_in': w(ks[2], (L, D_MODEL, IN_COLS), D_MODEL),
        'b_gate': 0.02 * jax.random.normal(ks[3], (L, N_BRANCH * D_MODEL), F32),
        'q_norm': gain(ks[4], (L, Q_LORA)),
        'w_uq': w(ks[5], (L, Q_LORA, MLA_HEADS * (MLA_NOPE + MLA_ROPE)), Q_LORA),
        'kv_norm': gain(ks[6], (L, KV_LORA)),
        'w_ukv': w(ks[7], (L, KV_LORA, MLA_HEADS * (MLA_NOPE + MLA_V)), KV_LORA),
        'w_o_mla': w(ks[8], (L, MLA_HEADS * MLA_V, D_MODEL), MLA_HEADS * MLA_V),
        'w_o_moba': w(ks[9], (L, MOBA_HEADS * MOBA_HD, D_MODEL), MOBA_HEADS * MOBA_HD),
        'w_out': w(ks[10], (L, D_MODEL, D_MODEL), D_MODEL),
        'ffn_norm': gain(ks[11], (L, D_MODEL)),
        'w_up': w(ks[12], (L, D_MODEL, 2 * D_FF), D_MODEL),
        'conv_w': w(ks[13], (L, CONV_W, 2 * D_FF), CONV_W),
        'conv_b': 0.02 * jax.random.normal(ks[14], (L, 2 * D_FF), F32),
        'w_down': w(ks[15], (L, D_FF, D_MODEL), D_FF),
        'final_norm': gain(ks[16], (D_MODEL,)),
    }

def second_block(x, attn_norm, w_in, b_gate, q_norm, w_uq, kv_norm, w_ukv, w_o_mla, w_o_moba,
              w_out, ffn_norm, w_up, conv_w, conv_b, w_down, final_norm):
    B, S, _ = x.shape
    pos = jnp.arange(S)
    for l in range(DEPTH_2):
        h = rmsnorm(x, attn_norm[l])
        proj = h @ w_in[l]
        q_lat = proj[..., OFF_QLAT:OFF_KVLAT]
        kv_lat = proj[..., OFF_KVLAT:OFF_KPE]
        k_pe = proj[..., OFF_KPE:OFF_MOBA]
        qkv_b = proj[..., OFF_MOBA:OFF_GATE]
        gates = jax.nn.sigmoid(proj[..., OFF_GATE:] + b_gate[l])
        g_a, g_b = gates[..., :D_MODEL], gates[..., D_MODEL:]

        q = (rmsnorm(q_lat, q_norm[l]) @ w_uq[l]).reshape(B, S, MLA_HEADS, MLA_NOPE + MLA_ROPE)
        q = q.transpose(0, 2, 1, 3)
        kv = (rmsnorm(kv_lat, kv_norm[l]) @ w_ukv[l]).reshape(B, S, MLA_HEADS, MLA_NOPE + MLA_V)
        kv = kv.transpose(0, 2, 1, 3)
        q_a = jnp.concatenate([q[..., :MLA_NOPE], rope(q[..., MLA_NOPE:], pos)], axis=-1)
        k_rot = jnp.broadcast_to(rope(k_pe[:, None], pos), (B, MLA_HEADS, S, MLA_ROPE))
        k_a = jnp.concatenate([kv[..., :MLA_NOPE], k_rot], axis=-1)
        v_a = kv[..., MLA_NOPE:]
        y_a = causal_attention_blocks(q_a, k_a, v_a, (MLA_NOPE + MLA_ROPE) ** -0.5)
        y_a = y_a.transpose(0, 2, 1, 3).reshape(B, S, MLA_HEADS * MLA_V) @ w_o_mla[l]

        qkv = qkv_b.reshape(B, S, 3, MOBA_HEADS, MOBA_HD).transpose(2, 0, 3, 1, 4)
        y_b = moba_attention(rope(qkv[0], pos), rope(qkv[1], pos), qkv[2])
        y_b = y_b.transpose(0, 2, 1, 3).reshape(B, S, MOBA_HEADS * MOBA_HD) @ w_o_moba[l]

        x = x + (g_a * y_a + g_b * y_b) @ w_out[l]

        h = rmsnorm(x, ffn_norm[l])
        u = causal_dwconv(h @ w_up[l], conv_w[l], conv_b[l])
        x = x + (jax.nn.silu(u[..., :D_FF]) * u[..., D_FF:]) @ w_down[l]
    return rmsnorm(x, final_norm)


DEPTH_3 = 1

ATT_HEADS = 8
ATT_HEAD_DIM = 64
ATT_QK_WIDTH = ATT_HEADS * 2 * ATT_HEAD_DIM
ATT_V_WIDTH = ATT_HEADS * 2 * ATT_HEAD_DIM
SSD_EXPAND = 2
SSD_INNER = SSD_EXPAND * D_MODEL
SSD_HEAD_DIM = 64
SSD_HEADS = SSD_INNER // SSD_HEAD_DIM
SSD_GROUPS = 8
SSD_HEADS_PER_GROUP = SSD_HEADS // SSD_GROUPS
SSD_STATE = 128
SSD_CONV = 4
SSD_CONV_CH = SSD_INNER + 2 * SSD_GROUPS * SSD_STATE
SSD_CHUNK = 128
IN_SPLITS = (ATT_QK_WIDTH, ATT_QK_WIDTH, ATT_V_WIDTH, SSD_INNER, SSD_CONV_CH, SSD_HEADS, D_MODEL, D_MODEL)
IN_COLS_3 = sum(IN_SPLITS)
MOE_GROUPS = 8
MOE_EXPERTS_PER_GROUP = 8
MOE_EXPERTS = MOE_GROUPS * MOE_EXPERTS_PER_GROUP
MOE_TOP_K = 2
MOE_HIDDEN = 512
MOE_BLOCK = 128
NORM_EPS = 1e-6
SUBLN_EPS = 1e-5
SSD_NORM_EPS = 1e-5


def rms_norm_3(x, w, eps):
    xf = x.astype(jnp.float32)
    y = xf * lax.rsqrt(jnp.mean(xf * xf, axis=-1, keepdims=True) + eps)
    return (y * w.astype(jnp.float32)).astype(x.dtype)

def rotary_tables(positions):
    inv_freq = 1.0 / (ROPE_THETA ** (jnp.arange(0, ATT_HEAD_DIM, 2, dtype=jnp.float32) / ATT_HEAD_DIM))
    ang = positions.astype(jnp.float32)[..., None] * inv_freq
    return jnp.cos(ang), jnp.sin(ang)

def apply_rotary(t, cos, sin):
    c = cos[:, :, None, None, :]
    sn = sin[:, :, None, None, :]
    tf = t.astype(jnp.float32)
    t1, t2 = jnp.split(tf, 2, axis=-1)
    return jnp.concatenate([t1 * c - t2 * sn, t2 * c + t1 * sn], axis=-1).astype(t.dtype)

def diff_attention(q, k, v, lam):
    s = q.shape[1]
    scale = ATT_HEAD_DIM ** -0.5
    outs = []
    for blk in range(s // Q_BLOCK):
        q_lo = blk * Q_BLOCK
        q_hi = q_lo + Q_BLOCK
        scores = jnp.einsum('bqhcd,bkhcd->bhcqk', q[:, q_lo:q_hi], k[:, :q_hi],
                            preferred_element_type=jnp.float32) * scale
        causal = (q_lo + jnp.arange(Q_BLOCK))[:, None] >= jnp.arange(q_hi)[None, :]
        probs = jax.nn.softmax(jnp.where(causal, scores, -jnp.inf), axis=-1)
        weights = probs[:, :, 0] - lam * probs[:, :, 1]
        outs.append(jnp.einsum('bhqk,bkhe->bqhe', weights.astype(v.dtype), v[:, :q_hi]))
    return jnp.concatenate(outs, axis=1)

def causal_depthwise_conv(u, w, bias):
    out = lax.conv_general_dilated(u, w[:, None, :], window_strides=(1,), padding=[(SSD_CONV - 1, 0)],
                                   dimension_numbers=('NWC', 'WIO', 'NWC'),
                                   feature_group_count=u.shape[-1])
    return out + bias

def ssd_chunked_scan(xdt, a, bm, cm):
    b, s, g, r, p = xdt.shape
    n = bm.shape[-1]
    nc = s // SSD_CHUNK

    def to_chunks(t):
        return jnp.moveaxis(t.reshape(b, nc, SSD_CHUNK, *t.shape[2:]), 1, 0)

    causal = jnp.tril(jnp.ones((SSD_CHUNK, SSD_CHUNK), dtype=bool))

    def step(state, inp):
        xc, ac, bc, cc = inp
        cum = jnp.cumsum(ac, axis=1)
        cum_t = jnp.moveaxis(cum, 1, -1)
        seg = cum_t[..., :, None] - cum_t[..., None, :]
        decay = jnp.exp(jnp.where(causal, seg, -jnp.inf))
        cb = jnp.einsum('bign,bjgn->bgij', cc, bc)
        y_diag = jnp.einsum('bgij,bgrij,bjgrp->bigrp', cb, decay, xc)
        y_off = jnp.einsum('bign,bgrpn->bigrp', cc, state) * jnp.exp(cum)[..., None]
        total = cum[:, -1]
        w_tail = jnp.exp(total[:, None] - cum)
        new_state = state * jnp.exp(total)[..., None, None] + jnp.einsum('bjgn,bjgr,bjgrp->bgrpn', bc, w_tail, xc)
        return new_state, y_diag + y_off

    init = jnp.zeros((b, g, r, p, n), jnp.float32)
    _, ys = lax.scan(step, init, (to_chunks(xdt), to_chunks(a), to_chunks(bm), to_chunks(cm)))
    return jnp.moveaxis(ys, 0, 1).reshape(b, s, g, r, p)

def ssd_branch(z, xbc, dt_raw, conv_w, conv_b, dt_bias, a_log, d_skip, norm_w):
    b, s, _ = z.shape
    xbc = jax.nn.silu(causal_depthwise_conv(xbc, conv_w, conv_b))
    xs, bm, cm = jnp.split(xbc, [SSD_INNER, SSD_INNER + SSD_GROUPS * SSD_STATE], axis=-1)
    xs = xs.reshape(b, s, SSD_GROUPS, SSD_HEADS_PER_GROUP, SSD_HEAD_DIM).astype(jnp.float32)
    bm = bm.reshape(b, s, SSD_GROUPS, SSD_STATE).astype(jnp.float32)
    cm = cm.reshape(b, s, SSD_GROUPS, SSD_STATE).astype(jnp.float32)
    dt = jax.nn.softplus(dt_raw.astype(jnp.float32) + dt_bias.astype(jnp.float32))
    dt = dt.reshape(b, s, SSD_GROUPS, SSD_HEADS_PER_GROUP)
    a = -jnp.exp(a_log.astype(jnp.float32)).reshape(SSD_GROUPS, SSD_HEADS_PER_GROUP)
    dsk = d_skip.astype(jnp.float32).reshape(SSD_GROUPS, SSD_HEADS_PER_GROUP)
    y = ssd_chunked_scan(xs * dt[..., None], dt * a, bm, cm) + dsk[..., None] * xs
    y = y.reshape(b, s, SSD_INNER) * jax.nn.silu(z.astype(jnp.float32))
    yg = y.reshape(b, s, SSD_GROUPS, SSD_INNER // SSD_GROUPS)
    yg = yg * lax.rsqrt(jnp.mean(yg * yg, axis=-1, keepdims=True) + SSD_NORM_EPS)
    return (yg.reshape(b, s, SSD_INNER) * norm_w.astype(jnp.float32)).astype(z.dtype)

def hierarchical_moe(h, w_gr, b_gr, w_er, b_er, w_gate, w_up, w_down):
    b, s, d = h.shape
    t = h.reshape(-1, d)
    n_tok = t.shape[0]
    g_logits = jnp.matmul(t, w_gr).astype(jnp.float32) + b_gr.astype(jnp.float32)
    g_prob = jax.nn.softmax(g_logits, axis=-1)
    g_sel = jnp.argmax(g_logits, axis=-1)
    g_gate = jnp.take_along_axis(g_prob, g_sel[:, None], axis=-1)[:, 0]
    e_logits = (jnp.matmul(t, w_er).astype(jnp.float32) + b_er.astype(jnp.float32))
    e_logits = e_logits.reshape(n_tok, MOE_GROUPS, MOE_EXPERTS_PER_GROUP)
    e_sel_logits = jnp.take_along_axis(e_logits, g_sel[:, None, None], axis=1)[:, 0]
    top_v, top_i = lax.top_k(e_sel_logits, MOE_TOP_K)
    weights = g_gate[:, None] * jax.nn.softmax(top_v, axis=-1)
    eid = g_sel[:, None].astype(jnp.int32) * MOE_EXPERTS_PER_GROUP + top_i.astype(jnp.int32)
    n_assign = n_tok * MOE_TOP_K
    flat_e = eid.reshape(-1)
    flat_tok = jnp.repeat(jnp.arange(n_tok, dtype=jnp.int32), MOE_TOP_K)
    flat_w = weights.reshape(-1)
    order = jnp.argsort(flat_e)
    se, st, sw = flat_e[order], flat_tok[order], flat_w[order]
    counts = jnp.bincount(flat_e, length=MOE_EXPERTS)
    starts = jnp.cumsum(counts) - counts
    padded = ((counts + MOE_BLOCK - 1) // MOE_BLOCK) * MOE_BLOCK
    pad_end = jnp.cumsum(padded)
    pad_start = pad_end - padded
    dest = pad_start[se] + (jnp.arange(n_assign, dtype=jnp.int32) - starts[se])
    n_buf = n_assign + MOE_EXPERTS * MOE_BLOCK
    n_blocks = n_buf // MOE_BLOCK
    buf_tok = jnp.zeros((n_buf,), jnp.int32).at[dest].set(st)
    buf_w = jnp.zeros((n_buf,), jnp.float32).at[dest].set(sw)
    blk_expert = jnp.minimum(jnp.searchsorted(pad_end, jnp.arange(n_blocks) * MOE_BLOCK, side='right'),
                             MOE_EXPERTS - 1)
    xb = t[buf_tok].reshape(n_blocks, MOE_BLOCK, d)

    def expert_block(args):
        xblk, e = args
        hid = jax.nn.silu(xblk @ w_gate[e]) * (xblk @ w_up[e])
        return hid @ w_down[e]

    yb = lax.map(expert_block, (xb, blk_expert)).reshape(n_buf, d)
    out = jnp.zeros((n_tok, d), jnp.float32).at[buf_tok].add(yb.astype(jnp.float32) * buf_w[:, None])
    return out.astype(h.dtype).reshape(b, s, d)

def third_inputs(seed: int = 0) -> dict:
    key = jax.random.key(seed)
    ks = jax.random.split(key, 28)
    f32 = jnp.float32

    def normal(k, shape, scale):
        return jax.random.normal(k, shape, f32) * scale

    x = normal(ks[0], (BATCH, SEQ, D_MODEL), 1.0)
    positions = (jnp.arange(SEQ, dtype=jnp.int32)[None, :]
                 + jax.random.randint(ks[1], (BATCH, 1), 0, SEQ, dtype=jnp.int32))
    norm_mix_w = 1.0 + normal(ks[2], (DEPTH_3, D_MODEL), 0.02)
    w_in = normal(ks[3], (DEPTH_3, D_MODEL, IN_COLS_3), D_MODEL ** -0.5)
    conv_w = normal(ks[4], (DEPTH_3, SSD_CONV, SSD_CONV_CH), SSD_CONV ** -0.5)
    conv_b = normal(ks[5], (DEPTH_3, SSD_CONV_CH), 0.02)
    dt0 = jnp.exp(jax.random.uniform(ks[6], (DEPTH_3, SSD_HEADS), f32, math.log(1e-3), math.log(1e-1)))
    dt_bias = dt0 + jnp.log(-jnp.expm1(-dt0))
    a_log = jnp.log(jax.random.uniform(ks[7], (DEPTH_3, SSD_HEADS), f32, 1.0, 16.0))
    d_skip = 1.0 + normal(ks[8], (DEPTH_3, SSD_HEADS), 0.1)
    ssd_norm_w = 1.0 + normal(ks[9], (DEPTH_3, SSD_INNER), 0.02)
    lambda_q1 = normal(ks[10], (DEPTH_3, ATT_HEAD_DIM), 0.1)
    lambda_k1 = normal(ks[11], (DEPTH_3, ATT_HEAD_DIM), 0.1)
    lambda_q2 = normal(ks[12], (DEPTH_3, ATT_HEAD_DIM), 0.1)
    lambda_k2 = normal(ks[13], (DEPTH_3, ATT_HEAD_DIM), 0.1)
    subln_w = 1.0 + normal(ks[14], (DEPTH_3, 2 * ATT_HEAD_DIM), 0.02)
    w_branch_attn = normal(ks[15], (DEPTH_3, ATT_V_WIDTH, D_MODEL), ATT_V_WIDTH ** -0.5)
    w_branch_ssd = normal(ks[16], (DEPTH_3, SSD_INNER, D_MODEL), SSD_INNER ** -0.5)
    w_out = normal(ks[17], (DEPTH_3, D_MODEL, D_MODEL), D_MODEL ** -0.5)
    norm_ffn_w = 1.0 + normal(ks[18], (DEPTH_3, D_MODEL), 0.02)
    w_group_router = normal(ks[19], (DEPTH_3, D_MODEL, MOE_GROUPS), D_MODEL ** -0.5)
    b_group_router = normal(ks[20], (DEPTH_3, MOE_GROUPS), 0.01)
    w_expert_router = normal(ks[21], (DEPTH_3, D_MODEL, MOE_EXPERTS), D_MODEL ** -0.5)
    b_expert_router = normal(ks[22], (DEPTH_3, MOE_EXPERTS), 0.01)
    w_expert_gate = normal(ks[23], (DEPTH_3, MOE_EXPERTS, D_MODEL, MOE_HIDDEN), D_MODEL ** -0.5)
    w_expert_up = normal(ks[24], (DEPTH_3, MOE_EXPERTS, D_MODEL, MOE_HIDDEN), D_MODEL ** -0.5)
    w_expert_down = normal(ks[25], (DEPTH_3, MOE_EXPERTS, MOE_HIDDEN, D_MODEL), MOE_HIDDEN ** -0.5)
    final_norm_w = 1.0 + normal(ks[26], (D_MODEL,), 0.02)
    return {'x': x, 'positions': positions, 'norm_mix_w': norm_mix_w, 'w_in': w_in,
            'conv_w': conv_w, 'conv_b': conv_b, 'dt_bias': dt_bias, 'a_log': a_log, 'd_skip': d_skip,
            'ssd_norm_w': ssd_norm_w, 'lambda_q1': lambda_q1, 'lambda_k1': lambda_k1,
            'lambda_q2': lambda_q2, 'lambda_k2': lambda_k2, 'subln_w': subln_w,
            'w_branch_attn': w_branch_attn, 'w_branch_ssd': w_branch_ssd, 'w_out': w_out,
            'norm_ffn_w': norm_ffn_w, 'w_group_router': w_group_router, 'b_group_router': b_group_router,
            'w_expert_router': w_expert_router, 'b_expert_router': b_expert_router,
            'w_expert_gate': w_expert_gate, 'w_expert_up': w_expert_up, 'w_expert_down': w_expert_down,
            'final_norm_w': final_norm_w}

def third_block(x, positions, norm_mix_w, w_in, conv_w, conv_b, dt_bias, a_log, d_skip, ssd_norm_w,
              lambda_q1, lambda_k1, lambda_q2, lambda_k2, subln_w, w_branch_attn, w_branch_ssd, w_out,
              norm_ffn_w, w_group_router, b_group_router, w_expert_router, b_expert_router,
              w_expert_gate, w_expert_up, w_expert_down, final_norm_w):
    b, s, _ = x.shape
    cos, sin = rotary_tables(positions)
    split_at = [int(o) for o in np.cumsum(IN_SPLITS)[:-1]]
    for l in range(DEPTH_3):
        lam_init = 0.8 - 0.6 * math.exp(-0.3 * l)
        h = rms_norm_3(x, norm_mix_w[l], NORM_EPS)
        proj = h @ w_in[l]
        q, k, v, z, xbc, dt_raw, gate_a, gate_s = jnp.split(proj, split_at, axis=-1)
        q = apply_rotary(q.reshape(b, s, ATT_HEADS, 2, ATT_HEAD_DIM), cos, sin)
        k = apply_rotary(k.reshape(b, s, ATT_HEADS, 2, ATT_HEAD_DIM), cos, sin)
        v = v.reshape(b, s, ATT_HEADS, 2 * ATT_HEAD_DIM)
        lam = (jnp.exp(jnp.sum(lambda_q1[l].astype(jnp.float32) * lambda_k1[l].astype(jnp.float32)))
               - jnp.exp(jnp.sum(lambda_q2[l].astype(jnp.float32) * lambda_k2[l].astype(jnp.float32)))
               + lam_init)
        att = diff_attention(q, k, v, lam)
        att = (rms_norm_3(att, subln_w[l], SUBLN_EPS) * (1.0 - lam_init)).reshape(b, s, ATT_V_WIDTH)
        ssd = ssd_branch(z, xbc, dt_raw, conv_w[l], conv_b[l], dt_bias[l], a_log[l], d_skip[l], ssd_norm_w[l])
        merged = (jax.nn.sigmoid(gate_a) * (att @ w_branch_attn[l])
                  + jax.nn.sigmoid(gate_s) * (ssd @ w_branch_ssd[l]))
        x = x + merged @ w_out[l]
        h2 = rms_norm_3(x, norm_ffn_w[l], NORM_EPS)
        x = x + hierarchical_moe(h2, w_group_router[l], b_group_router[l], w_expert_router[l],
                                 b_expert_router[l], w_expert_gate[l], w_expert_up[l], w_expert_down[l])
    return rms_norm_3(x, final_norm_w, NORM_EPS)


def setup_inputs(seed=0):
    out = dict(first_inputs(seed))
    for name, value in second_inputs(seed + 1).items():
        if name != "x":
            out[name + "_2"] = value
    for name, value in third_inputs(seed + 2).items():
        if name != "x":
            out[name + "_3"] = value
    return out


def reference(
    x, norm_g, final_g, ffn_w_in, ffn_w_out, conv_w_pw1, conv_b_pw1, conv_w_dw, conv_b_dw,
    conv_ln_g, conv_ln_b, conv_w_pw2, conv_b_pw2, attn_w_qkv, attn_w_o, attn_norm_2, w_in_2,
    b_gate_2, q_norm_2, w_uq_2, kv_norm_2, w_ukv_2, w_o_mla_2, w_o_moba_2, w_out_2, ffn_norm_2,
    w_up_2, conv_w_2, conv_b_2, w_down_2, final_norm_2, positions_3, norm_mix_w_3, w_in_3,
    conv_w_3, conv_b_3, dt_bias_3, a_log_3, d_skip_3, ssd_norm_w_3, lambda_q1_3, lambda_k1_3,
    lambda_q2_3, lambda_k2_3, subln_w_3, w_branch_attn_3, w_branch_ssd_3, w_out_3, norm_ffn_w_3,
    w_group_router_3, b_group_router_3, w_expert_router_3, b_expert_router_3, w_expert_gate_3,
    w_expert_up_3, w_expert_down_3, final_norm_w_3,
):
    x = first_block(
        x, norm_g, final_g, ffn_w_in, ffn_w_out, conv_w_pw1, conv_b_pw1, conv_w_dw, conv_b_dw,
        conv_ln_g, conv_ln_b, conv_w_pw2, conv_b_pw2, attn_w_qkv, attn_w_o,
    )
    x = second_block(
        x, attn_norm_2, w_in_2, b_gate_2, q_norm_2, w_uq_2, kv_norm_2, w_ukv_2, w_o_mla_2,
        w_o_moba_2, w_out_2, ffn_norm_2, w_up_2, conv_w_2, conv_b_2, w_down_2, final_norm_2,
    )
    return third_block(
        x, positions_3, norm_mix_w_3, w_in_3, conv_w_3, conv_b_3, dt_bias_3, a_log_3, d_skip_3,
        ssd_norm_w_3, lambda_q1_3, lambda_k1_3, lambda_q2_3, lambda_k2_3, subln_w_3,
        w_branch_attn_3, w_branch_ssd_3, w_out_3, norm_ffn_w_3, w_group_router_3,
        b_group_router_3, w_expert_router_3, b_expert_router_3, w_expert_gate_3, w_expert_up_3,
        w_expert_down_3, final_norm_w_3,
    )


_drawn_inputs = setup_inputs


def setup_inputs(seed=0):
    import zlib

    import numpy as np

    out = dict(_drawn_inputs(seed))
    spreads = {}
    factors = {'attn_norm_2': 8.0,
     'b_gate_2': 8.0,
     'q_norm_2': 8.0,
     'w_uq_2': 8.0,
     'kv_norm_2': 8.0,
     'w_o_mla_2': 2.685,
     'w_o_moba_2': 2.929,
     'ffn_norm_2': 8.0,
     'conv_b_2': 8.0,
     'conv_b_3': 3.359,
     'ssd_norm_w_3': 3.728,
     'lambda_q1_3': 3.079,
     'lambda_k1_3': 3.336,
     'lambda_q2_3': 3.204,
     'lambda_k2_3': 5.418,
     'subln_w_3': 8.0,
     'norm_ffn_w_3': 2.777,
     'b_group_router_3': 5.216,
     'b_expert_router_3': 8.0,
     'final_norm_w_3': 2.75}
    for name, (base, spread) in spreads.items():
        noise = np.random.default_rng([zlib.crc32(name.encode()), seed]).standard_normal(out[name].shape)
        drawn = base * np.exp(spread * noise) if base else spread * noise
        out[name] = jnp.asarray(drawn.astype(out[name].dtype))
    for name, factor in factors.items():
        out[name] = (out[name] * factor).astype(out[name].dtype)
    return out
```

```python
from contextlib import ExitStack

import numpy as np
import concourse.bass as bass
from concourse import mybir

P = 128
T = 2
S = T * P
DM = 1024
KC = DM // P
FF = 2816
FC = FF // P
NSLOT = 4
SLOT = 4096
UNIT_INC = 192
LANES = 4
TRI = 3 * P
SLOTS = 128
NEXP, HID = 64, 512
NBLK = NEXP + 4
EPS6, EPS5 = 1e-6, 1e-5
NEG = -1e30

F32, I32 = mybir.dt.float32, mybir.dt.int32
ACT, ALU, AX = mybir.ActivationFunctionType, mybir.AluOpType, mybir.AxisListType.X



def constant_columns():
    r = np.arange(P)
    ident = np.eye(P)
    lt = (r[:, None] < r[None, :]).astype(np.float32)
    le = (r[:, None] <= r[None, :]).astype(np.float32)
    one = np.ones((P, P))
    no = np.where(r[None, :] <= r[:, None], 0.0, NEG)

    def rotation(half):
        m = np.zeros((P, P))
        for d in range(P):
            if d % (2 * half) < half:
                m[d + half, d] = -1.0
            else:
                m[d - half, d] = 1.0
        return m

    def angles(dim):
        inv = np.float32(10000.0) ** (-np.arange(0, dim, 2, dtype=np.float32) / np.float32(dim))
        inv = inv.astype(np.float32)
        ang = (np.arange(S, dtype=np.float32)[None, :] * inv[:, None]).astype(np.float32)
        ang = np.tile(ang, (P // (dim // 2), 1))
        return np.cos(ang), np.sin(ang)

    inv3 = (np.float32(1.0) / (np.float32(10000.0) ** (np.arange(0, 64, 2, dtype=np.float32) / np.float32(64)))).astype(np.float32)
    cos128, sin128 = angles(128)
    cos64, sin64 = angles(64)
    return {
        "ident": ident, "ones": one, "mean": one / DM, "gt": lt.T, "lt": lt, "le": le,
        "mask_lt": np.concatenate([lt, one, lt], 1),
        "mask_le": np.concatenate([le, one, le], 1),
        "causal_add": np.concatenate([no, 0 * one, no], 1),
        "rot128": rotation(64), "rot64": rotation(32),
        "cos128": cos128, "sin128": sin128, "cos64": cos64, "sin64": sin64,
        "inv_freq": np.tile(inv3, 4)[:, None],
        "iota": np.tile(r.astype(np.float32), (P, 1)), "row": r[:, None],
    }


CONST = {}
_at = 0
_parts = []
for _name, _a in constant_columns().items():
    CONST[_name] = (_at, _at + _a.shape[1])
    _at += _a.shape[1]
    _parts.append(np.asarray(_a, np.float32))
CONST_ARRAY = np.ascontiguousarray(np.concatenate(_parts, 1))

PARAM_NAMES = ["norm_g", "conv_b_pw1", "conv_w_dw", "conv_b_dw", "conv_ln_g", "conv_ln_b",
               "attn_norm_2", "b_gate_2", "q_norm_2", "kv_norm_2", "ffn_norm_2", "conv_w_2", "conv_b_2",
               "norm_mix_w_3", "conv_w_3", "conv_b_3", "norm_ffn_w_3", "ssd_norm_w_3", "subln_w_3"]
PARAM_SIZES = [6 * DM, 2 * DM, 31 * DM, DM, DM, DM,
               DM, 2 * DM, 384, 256, DM, 3 * 2 * FF, 2 * FF,
               DM, 4 * 4096, 4096, DM, 2048, 128]
PARAM = {}
_at = 0
for _name, _n in zip(PARAM_NAMES, PARAM_SIZES):
    PARAM[_name] = _at
    _at += _n // P
N_PARAM = _at

ROW_NAMES = ["final_g", "final_norm_2", "final_norm_w_3", "conv_b_pw2", "b_group_router_3", "b_expert_router_3",
             "dt_bias_3", "a_log_3", "d_skip_3", "lambda_q1_3", "lambda_k1_3", "lambda_q2_3", "lambda_k2_3"]
ROW_SIZES = [DM, DM, DM, DM, 8, 64, 32, 32, 32, 64, 64, 64, 64]
ROW = {}
_at = 0
for _name, _n in zip(ROW_NAMES, ROW_SIZES):
    ROW[_name] = (_at, _at + _n)
    _at += _n
N_ROW = _at

WEIGHTS = ["ffn_w_in", "ffn_w_out", "conv_w_pw1", "conv_w_pw2", "attn_w_qkv", "attn_w_o", "w_in_2", "w_uq_2",
           "w_ukv_2", "w_o_mla_2", "w_o_moba_2", "w_out_2", "w_up_2", "w_down_2", "w_in_3", "w_branch_attn_3",
           "w_branch_ssd_3", "w_out_3", "w_group_router_3", "w_expert_router_3", "w_expert_gate_3",
           "w_expert_up_3", "w_expert_down_3"]


class Chain:

    def __init__(self, eng, sem):
        self.eng, self.sem = eng, sem
        self.count = {}
        self.loop = None

    def credit(self, sem, n):
        self.count[sem.name] = n

    def __call__(self, ins, done=None):
        sem = done if done is not None else self.sem
        ins.then_inc(sem, 1)
        if self.loop is None:
            self.count[sem.name] = self.count.get(sem.name, 0) + 1
            self.eng.wait_ge(sem, self.count[sem.name])
        else:
            i, per, k = self.loop
            k[sem.name] = k.get(sem.name, 0) + 1
            self.eng.wait_ge(sem, i * per[sem.name] + (self.count.get(sem.name, 0) + k[sem.name]))

    def enter(self, i, own, others):
        self.loop = (i, {self.sem.name: own, **{sem.name: n for sem, n in others}}, {})

    def leave(self, count):
        _, per, k = self.loop
        assert k == per, (k, per)
        for name, n in per.items():
            self.count[name] = self.count.get(name, 0) + n * count
        self.loop = None


class Core:

    def __init__(self, nc, ctx, arg):
        self.nc, self.ctx, self.arg = nc, ctx, arg
        sb, ps = self.sb, self.ps = self._sbuf, self._psum
        self.x = sb("x", [P, T, DM])
        self.xn = sb("xn", [P, T, DM])
        self.hT = sb("hT", [P, KC, S])
        self.ring = sb("ring", [P, NSLOT, SLOT])
        self.big = sb("big", [P, 24, S])
        self.par = sb("par", [P, N_PARAM])
        self.row = sb("row", [P, N_ROW])
        self.con = sb("con", [P, CONST_ARRAY.shape[1]])
        self.wk = sb("wk", [P, 9216])
        self.ss = sb("ss", [P, 16])
        self.bank = ps("bank", [P, 8, 512])
        self.w_loaded = [self.sem(f"w_loaded{i}") for i in range(NSLOT)]
        self.w_used = self.sem("w_used")
        self.barrier = self.sem("barrier")
        self.setup_loaded = self.sem("setup_loaded")
        self.chain_sem = {e: self.sem(f"{e}_chain") for e in ("act", "dve", "pool")}
        self.units = 0
        self.turns, self.named = {}, {}

    def _sbuf(self, name, shape, dt=F32):
        return self.ctx.enter_context(self.nc.sbuf_tensor(name, shape, dt))

    def _psum(self, name, shape, dt=F32):
        return self.ctx.enter_context(self.nc.psum_tensor(name, shape, dt))

    def sem(self, name):
        return self.ctx.enter_context(self.nc.semaphore(name))

    def c(self, name):
        a, b = CONST[name]
        return self.con[:, a:b]

    def p(self, name, n, k=1):
        a = PARAM[name] + n
        return self.par[:, a:a + k]

    def r(self, name):
        a, b = ROW[name]
        return self.row[:, a:b]

    def take_units(self, n):
        u = self.units
        self.units += n
        return u

    def slot(self, slot, off, a, b):
        return self.ring[:, slot, off:off + a * b].rearrange("p (a b) -> p a b", a=a)


def rows_of(w, c0, n, k0=0, k=None):
    rows = w[k0 * P:(k0 + k) * P, c0:c0 + n] if k else w[:, c0:c0 + n]
    return rows.rearrange("(a p) n -> p a n", p=P)


class Stage:
    TOTAL = {}
    UNITS = 0

    def __init__(self, k, name):
        self.k, self.name = k, name
        self.kind = type(self).__name__
        self.turn = k.turns.get(self.kind, 0)
        k.turns[self.kind] = self.turn + 1
        self.base = {}
        self.name_sems(self.shared_sem)
        self.u0 = k.take_units(self.UNITS)

    def name_sems(self, sem):
        pass

    def shared_sem(self, name):
        full = f"{self.kind}_{name}"
        if full not in self.k.named:
            self.k.named[full] = self.k.sem(full)
        self.base[full] = self.turn * self.TOTAL[name] if self.turn else 0
        return self.k.named[full]

    def at(self, sem, value):
        return value + self.base[sem.name]

    def slot_of(self, j):
        return (self.u0 + j) % NSLOT

    def loaded(self, j):
        return self.k.w_loaded[self.slot_of(j)]

    def loads(self, j, i=0):
        return (i + (self.u0 + j) // NSLOT + 1) * UNIT_INC

    def freed(self, j, i=0):
        return i * NSLOT + self.u0 + j + 1

    def used(self, j):
        return j + self.u0 + NSLOT + 1

    def sp(self, sp):
        pass

    def pe(self, pe):
        pass

    def act(self, act, chain):
        pass

    def dve(self, dve, chain):
        pass

    def pool(self, pool, chain):
        pass


class Setup(Stage):

    def act(self, act, chain):
        k = self.k
        act.dma_start(k.x[:, :, :], k.arg["x"].rearrange("a (t p) n -> p (a t) n", p=P)).then_inc(k.setup_loaded, 16)
        act.dma_start(k.con[:, :], k.arg["constants"]).then_inc(k.setup_loaded, 16)
        act.dma_start(k.par[:, :], k.arg["params"]).then_inc(k.setup_loaded, 16)
        act.dma_start(k.row[:, :], k.arg["rows"].to_broadcast([P, N_ROW])).then_inc(k.setup_loaded, 16)
        act.wait_ge(k.setup_loaded, 64)


class Norm(Stage):
    TOTAL = {"squared": T, "mean_ready": 1, "root_ready": 1, "xn_ready": T, "turned": 2 * T}

    def name_sems(self, sem):
        self.squared = sem("squared")
        self.mean_ready = sem("mean_ready")
        self.root_ready = sem("root_ready")
        self.xn_ready = sem("xn_ready")
        self.turned = sem("turned")

    def __init__(self, k, name, gain):
        super().__init__(k, name)
        self.gain = gain

    def act(self, act, chain):
        k, nc = self.k, self.k.nc
        for t in range(T):
            chain(nc.scalar.activation(k.wk[:, t * DM:(t + 1) * DM], k.x[:, t, :], ACT.Square,
                                       accum_out=k.ss[:, t:t + 1]), self.squared)
        act.wait_ge(self.mean_ready, self.at(self.mean_ready, 1))
        chain(nc.scalar.activation(k.ss[:, 4:6], k.ss[:, 2:4], ACT.Sqrt), self.root_ready)

    def dve(self, dve, chain):
        k, nc = self.k, self.k.nc
        dve.wait_ge(self.squared, self.at(self.squared, T))
        chain(nc.vector.tensor_scalar(k.ss[:, 2:4], k.ss[:, 0:2], 1.0 / DM, EPS6, ALU.mult, ALU.add), self.mean_ready)
        dve.wait_ge(self.root_ready, self.at(self.root_ready, 1))
        chain(nc.vector.reciprocal(k.ss[:, 6:8], k.ss[:, 4:6]))
        for t in range(T):
            nc.vector.tensor_scalar(k.xn[:, t, :], k.x[:, t, :], k.ss[:, 6 + t:7 + t], None,
                                    ALU.mult).then_inc(self.xn_ready, 1)
        for t in range(T):
            for h in range(2):
                dve.wait_ge(self.turned, self.at(self.turned, 2 * t + h + 1))
                g = k.p(self.gain[0], self.gain[1] + 4 * h, 4).rearrange("p (a b) -> p a b", b=1).to_broadcast([P, 4, P])
                last = nc.vector.tensor_tensor(k.hT[:, 4 * h:4 * h + 4, t * P:(t + 1) * P],
                                               k.bank[:, 2 * t + h, :].rearrange("p (a b) -> p a b", a=4), g, ALU.mult)
        chain(last)

    def pe(self, pe):
        k, nc = self.k, self.k.nc
        for t in range(T):
            pe.wait_ge(self.xn_ready, self.at(self.xn_ready, t + 1))
            for c in range(KC):
                last = nc.tensor.transpose(k.bank[:, 2 * t + c // 4, (c % 4) * P:(c % 4 + 1) * P],
                                           k.xn[:, t, c * P:(c + 1) * P], k.c("ident"))
                if c % 4 == 3:
                    last.then_inc(self.turned, 1)


class FinalNorm(Stage):
    TOTAL = {"squared": T, "mean_ready": 1, "root_ready": 1}

    def name_sems(self, sem):
        self.squared = sem("squared")
        self.mean_ready = sem("mean_ready")
        self.root_ready = sem("root_ready")

    def __init__(self, k, name, row):
        super().__init__(k, name)
        self.row = row

    def act(self, act, chain):
        k, nc = self.k, self.k.nc
        for t in range(T):
            chain(nc.scalar.activation(k.wk[:, t * DM:(t + 1) * DM], k.x[:, t, :], ACT.Square,
                                       accum_out=k.ss[:, t:t + 1]), self.squared)
        act.wait_ge(self.mean_ready, self.at(self.mean_ready, 1))
        chain(nc.scalar.activation(k.ss[:, 4:6], k.ss[:, 2:4], ACT.Sqrt), self.root_ready)

    def dve(self, dve, chain):
        k, nc = self.k, self.k.nc
        dve.wait_ge(self.squared, self.at(self.squared, T))
        chain(nc.vector.tensor_scalar(k.ss[:, 2:4], k.ss[:, 0:2], 1.0 / DM, EPS6, ALU.mult, ALU.add), self.mean_ready)
        dve.wait_ge(self.root_ready, self.at(self.root_ready, 1))
        chain(nc.vector.reciprocal(k.ss[:, 6:8], k.ss[:, 4:6]))
        for t in range(T):
            chain(nc.vector.scalar_tensor_tensor(k.x[:, t, :], k.x[:, t, :], k.ss[:, 6 + t:7 + t], k.r(self.row),
                                                 ALU.mult, ALU.mult))


class GatedUp(Stage):
    UNITS = FC // 2
    TOTAL = {"up_ready": FC // 2, "gate_ready": FC, "hid_done": FC + 4}

    def name_sems(self, sem):
        self.up_ready = sem("up_ready")
        self.gate_ready = sem("gate_ready")
        self.hid_done = sem("hid_done")

    def __init__(self, k, name, w):
        super().__init__(k, name)
        self.w = w

    def panels(self, eng, body):
        n = self.UNITS
        with eng.Fori(0, n // NSLOT) as i:
            for s in range(NSLOT):
                body(i * NSLOT + s, s, i)
        for j in range(n // NSLOT * NSLOT, n):
            body(j, j, 0)

    def sp(self, sp):
        def body(j, s, i):
            slot = self.slot_of(s)
            parts = [(self.k.slot(slot, 0, KC, 512)[:, :, h * 256:(h + 1) * 256],
                      self.w[:, bass.ds(j * 256 + h * FF, 256)].rearrange("(a p) n -> p a n", p=P)) for h in range(2)]
            sp.wait_ge(self.k.w_used, self.freed(s, i))
            for dst, src in parts:
                sp.dma_start(dst, src).then_inc(self.loaded(s), UNIT_INC // len(parts))
        self.panels(sp, body)

    def pe(self, pe):
        k, nc = self.k, self.k.nc

        def body(j, s, i):
            pe.wait_ge(self.loaded(s), self.loads(s, i))
            w = k.slot(self.slot_of(s), 0, KC, 512)
            for m in range(2):
                b = (2 * s + m) % 4
                pe.wait_ge(self.hid_done, self.at(self.hid_done, j * 2 + m + 1))
                for h in range(2):
                    for c in range(KC):
                        last = nc.tensor.matmul(k.bank[:, b, h * S:(h + 1) * S],
                                                w[:, c, h * 256 + m * P:h * 256 + (m + 1) * P], k.hT[:, c, :],
                                                start=c == 0, stop=c == KC - 1)
                last.then_inc(k.w_used if m else self.up_ready, 1)
        pe.sem_inc(self.hid_done, 4)
        self.panels(pe, body)

    def act(self, act, chain):
        k, nc = self.k, self.k.nc

        def body(j, s, i):
            for m in range(2):
                b = (2 * s + m) % 4
                if m:
                    act.wait_ge(k.w_used, self.used(j))
                else:
                    act.wait_ge(self.up_ready, self.at(self.up_ready, j + 1))
                act.wait_ge(self.hid_done, self.at(self.hid_done, j * 2 + m + 3))
                nc.scalar.activation(k.wk[:, m * S:(m + 1) * S], k.bank[:, b, 0:S], ACT.Silu)\
                  .then_inc(self.gate_ready, 1)
        self.panels(act, body)

    def dve(self, dve, chain):
        k, nc = self.k, self.k.nc

        def body(j, s, i):
            for m in range(2):
                b = (2 * s + m) % 4
                dve.wait_ge(self.gate_ready, self.at(self.gate_ready, j * 2 + m + 1))
                nc.vector.tensor_tensor(k.big[:, bass.ds(j * 2 + m, 1), :].rearrange("p a n -> p (a n)"),
                                        k.bank[:, b, S:2 * S], k.wk[:, m * S:(m + 1) * S], ALU.mult)\
                  .then_inc(self.hid_done, 1)
        self.panels(dve, body)


class ConvUp(GatedUp):
    PAD = S + 2

    def name_sems(self, sem):
        self.up_ready = sem("up_ready")
        self.copied = sem("copied")
        self.conv_done = sem("conv_done")
        self.gate_ready = sem("gate_ready")
        self.hid_done = sem("hid_done")
        self.pads_zero = sem("pads_zero")

    def padded(self, m, h):
        a = (2 * m + h) * self.PAD
        return self.k.wk[:, a:a + self.PAD]

    def acc(self, m, h):
        a = 4 * self.PAD + (2 * m + h) * S
        return self.k.wk[:, a:a + S]

    def taps(self, c, h, j):
        a = PARAM["conv_w_2"] + j * 2 * FC + h * FC
        return self.k.par[:, bass.ds(c + a, 1)]

    def act(self, act, chain):
        k, nc = self.k, self.k.nc
        act.wait_ge(self.pads_zero, 4)

        def body(j, s, i):
            for m in range(2):
                b = (2 * s + m) % 4
                if m:
                    act.wait_ge(k.w_used, self.used(j))
                else:
                    act.wait_ge(self.up_ready, self.at(self.up_ready, j + 1))
                act.wait_ge(self.conv_done, j * 2 + m + 1)
                for h in range(2):
                    nc.scalar.activation(self.padded(m, h)[:, 2:], k.bank[:, b, h * S:(h + 1) * S], ACT.Copy)\
                      .then_inc(self.copied, 1)
                act.wait_ge(self.conv_done, j * 2 + m + 3)
                nc.scalar.activation(k.wk[:, 6000 + m * S:6000 + (m + 1) * S], self.acc(m, 0), ACT.Silu)\
                  .then_inc(self.gate_ready, 1)
        self.panels(act, body)

    def dve(self, dve, chain):
        k, nc = self.k, self.k.nc
        for m in range(2):
            for h in range(2):
                nc.vector.memset(self.padded(m, h)[:, 0:2], 0.0).then_inc(self.pads_zero, 1)
        dve.sem_inc(self.conv_done, 2)
        chain.credit(self.conv_done, 2)
        chain.credit(self.hid_done, 4)
        n_full = self.UNITS // NSLOT

        def body(j, s, i):
            for m in range(2):
                c = j * 2 + m
                dve.wait_ge(self.copied, j * 4 + 2 * m + 2)
                for h in range(2):
                    pad, acc = self.padded(m, h), self.acc(m, h)
                    chain(nc.vector.tensor_scalar(acc, pad[:, 2:2 + S], self.taps(c, h, 2),
                                                  k.par[:, bass.ds(c + PARAM["conv_b_2"] + h * FC, 1)], ALU.mult, ALU.add))
                    for tap in (1, 0):
                        chain(nc.vector.scalar_tensor_tensor(acc, pad[:, tap:tap + S], self.taps(c, h, tap), acc,
                                                             ALU.mult, ALU.add),
                              self.conv_done if (tap == 0 and h == 1) else None)
                dve.wait_ge(self.gate_ready, c + 1)
                chain(nc.vector.tensor_tensor(k.big[:, bass.ds(c, 1), :].rearrange("p a n -> p (a n)"), self.acc(m, 1),
                                              k.wk[:, 6000 + m * S:6000 + (m + 1) * S], ALU.mult), self.hid_done)

        with dve.Fori(0, n_full) as i:
            chain.enter(i, NSLOT * 2 * 5, [(self.conv_done, NSLOT * 2), (self.hid_done, NSLOT * 2)])
            for s in range(NSLOT):
                body(i * NSLOT + s, s, i)
        chain.leave(n_full)
        for j in range(n_full * NSLOT, self.UNITS):
            body(j, j, 0)


class Project(Stage):

    def __init__(self, k, name, src, chunks, w, scale=1.0, bias=None):
        self.UNITS = -(-chunks // 4)
        super().__init__(k, name)
        self.src, self.chunks, self.w, self.scale, self.bias = src, chunks, w, scale, bias

    def sp(self, sp):
        for j in range(self.UNITS):
            n = min(4, self.chunks - 4 * j)
            parts = [(self.k.slot(self.slot_of(j), 0, n, DM), rows_of(self.w, 0, DM, 4 * j, n))]
            sp.wait_ge(self.k.w_used, self.freed(j))
            for dst, src in parts:
                sp.dma_start(dst, src).then_inc(self.loaded(j), UNIT_INC // len(parts))

    def pe(self, pe):
        k, nc = self.k, self.k.nc
        for j in range(self.UNITS):
            pe.wait_ge(self.loaded(j), self.loads(j))
            n = min(4, self.chunks - 4 * j)
            w = k.slot(self.slot_of(j), 0, n, DM)
            for c in range(n):
                for t in range(T):
                    for h in range(2):
                        if j == 0 and c == 0 and self.bias:
                            nc.tensor.matmul(k.bank[:, 4 + 2 * t + h, :], k.c("ones")[0:1, :],
                                             k.r(self.bias)[0:1, h * 512:(h + 1) * 512], start=True, stop=False)
                        last = nc.tensor.matmul(k.bank[:, 4 + 2 * t + h, :], self.src[:, 4 * j + c, t * P:(t + 1) * P],
                                                w[:, c, h * 512:(h + 1) * 512],
                                                start=j + c == 0 and not self.bias, stop=4 * j + c == self.chunks - 1)
            last.then_inc(k.w_used, 1)

    def dve(self, dve, chain):
        k, nc = self.k, self.k.nc
        dve.wait_ge(self.k.w_used, self.used(self.UNITS - 1))
        for t in range(T):
            for h in range(2):
                x = k.x[:, t, h * 512:(h + 1) * 512]
                nc.vector.scalar_tensor_tensor(x, k.bank[:, 4 + 2 * t + h, :], self.scale, x, ALU.mult, ALU.add)


class ConvGlu(Stage):
    UNITS = 4
    TAPS = 31
    W = S + 30

    def name_sems(self, sem):
        self.up_ready = sem("up_ready")
        self.gate_ready = sem("gate_ready")
        self.u_ready = sem("u_ready")

    def u(self, c):
        return self.k.wk[:, c * self.W:(c + 1) * self.W]

    def sp(self, sp):
        w = self.k.arg["conv_w_pw1"][0]
        for j in range(4):
            parts = [(self.k.slot(self.slot_of(j), 0, KC, 512)[:, :, h * 256:(h + 1) * 256],
                               rows_of(w, h * DM + j * 256, 256)) for h in range(2)]
            sp.wait_ge(self.k.w_used, self.freed(j))
            for dst, src in parts:
                sp.dma_start(dst, src).then_inc(self.loaded(j), UNIT_INC // len(parts))

    def pe(self, pe):
        k, nc = self.k, self.k.nc
        for j in range(4):
            pe.wait_ge(self.loaded(j), self.loads(j))
            w = k.slot(self.slot_of(j), 0, KC, 512)
            for m in range(2):
                c = 2 * j + m
                if c >= 4:
                    pe.wait_ge(self.u_ready, c - 3)
                for h in range(2):
                    for q in range(KC):
                        last = nc.tensor.matmul(k.bank[:, c % 4, h * S:(h + 1) * S],
                                                w[:, q, h * 256 + m * P:h * 256 + (m + 1) * P], k.hT[:, q, :],
                                                start=q == 0, stop=q == KC - 1)
                last.then_inc(k.w_used if m else self.up_ready, 1)

    def act(self, act, chain):
        k, nc = self.k, self.k.nc
        for c in range(KC):
            if c % 2:
                act.wait_ge(self.k.w_used, self.used(c // 2))
            else:
                act.wait_ge(self.up_ready, c // 2 + 1)
            nc.scalar.activation(k.big[:, 16 + c, :], k.bank[:, c % 4, S:2 * S], ACT.Sigmoid,
                                 bias=k.p("conv_b_pw1", KC + c)).then_inc(self.gate_ready, 1)

    def dve(self, dve, chain):
        k, nc = self.k, self.k.nc
        for c in range(KC):
            chain(nc.vector.memset(self.u(c)[:, 0:30], 0.0))
        for c in range(KC):
            dve.wait_ge(self.gate_ready, c + 1)
            chain(nc.vector.scalar_tensor_tensor(self.u(c)[:, 30:], k.bank[:, c % 4, 0:S], k.p("conv_b_pw1", c),
                                                 k.big[:, 16 + c, :], ALU.add, ALU.mult), self.u_ready)


class DepthConv(Stage):
    W, TAPS, ND = ConvGlu.W, 31, 4
    FOR_DVE = 4

    def name_sems(self, sem):
        self.conv_dve = sem("conv_dve")
        self.diag_ready = sem("diag_ready")
        self.diag_used = sem("diag_used")
        self.conv_act = sem("conv_act")
        self.mean_ready = sem("mean_ready")
        self.centered = sem("centered")
        self.squared = sem("squared")
        self.var_ready = sem("var_ready")
        self.std_ready = sem("std_ready")
        self.root_ready = sem("root_ready")
        self.scaled = sem("scaled")

    def pe(self, pe):
        k, nc = self.k, self.k.nc
        diag = k.big
        n = 0
        for c in range(self.FOR_DVE, KC):
            for j in range(self.TAPS):
                pe.wait_ge(self.diag_ready, n + 1)
                nc.tensor.matmul(k.bank[:, c - self.FOR_DVE, 0:S], k.big[:, 16 + n % self.ND, 0:P],
                                 k.wk[:, c * self.W + j:c * self.W + j + S],
                                 start=j == 0, stop=j == self.TAPS - 1).then_inc(self.diag_used, 1)
                n += 1
        pe.wait_ge(self.conv_dve, self.TAPS * self.FOR_DVE)
        pe.wait_ge(self.conv_act, KC - self.FOR_DVE)
        for c in range(KC):
            last = nc.tensor.matmul(k.bank[:, 4, 0:S], k.c("mean"), k.big[:, c, :], start=c == 0, stop=c == KC - 1)
        last.then_inc(self.mean_ready, 1)
        pe.wait_ge(self.squared, 1)
        for c in range(KC):
            last = nc.tensor.matmul(k.bank[:, 5, 0:S], k.c("mean"), k.big[:, 8 + c, :], start=c == 0, stop=c == KC - 1)
        last.then_inc(self.var_ready, 1)

    def act(self, act, chain):
        k, nc = self.k, self.k.nc
        n = 0
        for c in range(self.FOR_DVE, KC):
            for j in range(self.TAPS):
                if n >= self.ND:
                    act.wait_ge(self.diag_used, n - self.ND + 1)
                nc.scalar.activation(k.big[:, 16 + n % self.ND, 0:P], k.c("ident"), ACT.Copy,
                                     scale=k.p("conv_w_dw", j * KC + c)).then_inc(self.diag_ready, 1)
                n += 1
            act.wait_ge(self.diag_used, n)
            chain(nc.scalar.activation(k.big[:, c, :], k.bank[:, c - self.FOR_DVE, 0:S], ACT.Identity,
                                       bias=k.p("conv_b_dw", c)), self.conv_act)
        act.wait_ge(self.centered, 1)
        chain(nc.scalar.activation(k.big[:, 8:16, :], k.big[:, 0:8, :], ACT.Square), self.squared)
        act.wait_ge(self.std_ready, 1)
        chain(nc.scalar.activation(k.big[:, 16, :], k.big[:, 17, :], ACT.Sqrt), self.root_ready)
        act.wait_ge(self.scaled, 1)
        for c in range(KC):
            nc.scalar.activation(k.big[:, c, :], k.big[:, c, :], ACT.Silu,
                                 bias=k.p("conv_ln_b", c), scale=k.p("conv_ln_g", c))

    def dve(self, dve, chain):
        k, nc = self.k, self.k.nc
        n = 0
        for j in range(self.TAPS):
            for c in range(self.FOR_DVE):
                u, w = k.wk[:, c * self.W + j:c * self.W + j + S], k.p("conv_w_dw", j * KC + c)
                if j == 0:
                    ins = nc.vector.tensor_scalar(k.big[:, c, :], u, w, k.p("conv_b_dw", c), ALU.mult, ALU.add)
                else:
                    dve.wait_ge(self.conv_dve, n - self.FOR_DVE + 1)
                    ins = nc.vector.scalar_tensor_tensor(k.big[:, c, :], u, w, k.big[:, c, :], ALU.mult, ALU.add)
                ins.then_inc(self.conv_dve, 1)
                n += 1
        dve.wait_ge(self.mean_ready, 1)
        mean = k.bank[:, 4:5, 0:S].to_broadcast([P, KC, S])
        chain(nc.vector.tensor_tensor(k.big[:, 0:8, :], k.big[:, 0:8, :], mean, ALU.subtract), self.centered)
        dve.wait_ge(self.var_ready, 1)
        chain(nc.vector.tensor_scalar(k.big[:, 17, :], k.bank[:, 5, 0:S], EPS5, None, ALU.add), self.std_ready)
        dve.wait_ge(self.root_ready, 1)
        chain(nc.vector.reciprocal(k.big[:, 18, :], k.big[:, 16, :]))
        chain(nc.vector.tensor_tensor(k.big[:, 0:8, :], k.big[:, 0:8, :], k.big[:, 18:19, :].to_broadcast([P, KC, S]),
                                      ALU.mult), self.scaled)


class Heads(Stage):
    G = 8
    UNITS = 8
    QT, KT, V = 0, 512, 1024
    FREE = 1536

    def __init__(self, k, name, w, q0, k0, v0):
        super().__init__(k, name)
        self.w, self.cols = w, (q0, k0, v0)

    def buf(self, base, g):
        a = base + (g % 2) * S
        return self.k.wk[:, a:a + S]

    def sp(self, sp):
        for g in range(self.G):
            v = self.k.slot(self.slot_of(g), 0, KC, 384)
            parts = [(v[:, :, n * P:(n + 1) * P], rows_of(self.w, self.cols[n] + g * P, P))
                              for n in range(3)]
            sp.wait_ge(self.k.w_used, self.freed(g))
            for dst, src in parts:
                sp.dma_start(dst, src).then_inc(self.loaded(g), UNIT_INC // len(parts))

    def project_qk(self, pe, g):
        k, nc = self.k, self.k.nc
        pe.wait_ge(self.loaded(g), self.loads(g))
        w = k.slot(self.slot_of(g), 0, KC, 384)
        if g:
            pe.wait_ge(self.qk_taken, self.at(self.qk_taken, g))
        for n in range(2):
            for c in range(KC):
                last = nc.tensor.matmul(k.bank[:, 0, n * S:(n + 1) * S], w[:, c, n * P:(n + 1) * P], k.hT[:, c, :],
                                        start=c == 0, stop=c == KC - 1)
        last.then_inc(self.qk_ready, 1)

    def project_v(self, pe, g):
        k, nc = self.k, self.k.nc
        w = k.slot(self.slot_of(g), 0, KC, 384)
        if g:
            pe.wait_ge(self.v_taken, self.at(self.v_taken, g))
        for t in range(T):
            for c in range(KC):
                last = nc.tensor.matmul(k.bank[:, 1, t * P:(t + 1) * P], k.hT[:, c, t * P:(t + 1) * P],
                                        w[:, c, 2 * P:3 * P], start=c == 0, stop=c == KC - 1)
        last.then_inc(k.w_used, 1)

    def v_projected(self, g):
        return self.k.w_used, self.used(g)

    def attend(self, pe, g, probs, v, out, mm=None):
        nc = self.k.nc
        nc.tensor.matmul(out, v(0), probs[:, 0:S], start=True, stop=False, skip_group_check=True)
        return nc.tensor.matmul(out[:, P:S], v(1), probs[:, S:TRI], start=False, stop=True, skip_group_check=True)


class Stick(Heads):
    ABS, E, LB, L1, PR = Heads.FREE, Heads.FREE + 768, Heads.FREE + 1536, Heads.FREE + 2304, Heads.FREE + 3072

    def name_sems(self, sem):
        self.qk_ready = sem("qk_ready")
        self.qk_taken = sem("qk_taken")
        self.v_taken = sem("v_taken")
        self.z_ready = sem("z_ready")
        self.abs_ready = sem("abs_ready")
        self.log_ready = sem("log_ready")
        self.l1_ready = sem("l1_ready")
        self.suf_ready = sem("suf_ready")
        self.logp_ready = sem("logp_ready")
        self.expd = sem("expd")
        self.p_ready = sem("p_ready")
        self.o_ready = sem("o_ready")
        self.o_taken = sem("o_taken")

    def two(self, base):
        return self.k.wk[:, base:base + 2 * TRI].rearrange("p (h n) -> p h n", h=2)

    def pe(self, pe):
        k, nc = self.k, self.k.nc
        self.project_qk(pe, 0)
        self.project_v(pe, 0)
        for g in range(self.G):
            q, kk, v = self.buf(self.QT, g), self.buf(self.KT, g), self.buf(self.V, g)
            pe.wait_ge(self.qk_taken, g + 1)
            if g:
                pe.wait_ge(self.l1_ready, g)
            for h in range(2):
                r = slice(64 * h, 64 * h + 64)
                nc.tensor.matmul(k.bank[:, 2 + h, 0:S], kk[r, 0:P], q[r, :], start=True, stop=True)
                last = nc.tensor.matmul(k.bank[:, 2 + h, S:TRI], kk[r, P:S], q[r, P:S], start=True, stop=True)
            last.then_inc(self.z_ready, 1)
            if g + 1 < self.G:
                self.project_qk(pe, g + 1)
            pe.wait_ge(self.l1_ready, g + 1)
            if g:
                pe.wait_ge(self.logp_ready, g)
            l1 = self.two(self.L1)
            for h in range(2):
                nc.tensor.matmul(k.bank[:, 4 + h, 0:S], k.c("gt"), l1[:, h, 0:S], start=True, stop=False,
                                 skip_group_check=True)
                nc.tensor.matmul(k.bank[:, 4 + h, P:S], k.c("ones"), l1[:, h, S:TRI], start=False, stop=True,
                                 skip_group_check=True)
                last = nc.tensor.matmul(k.bank[:, 4 + h, S:TRI], k.c("gt"), l1[:, h, S:TRI], start=True, stop=True)
            last.then_inc(self.suf_ready, 1)
            if g + 1 < self.G:
                self.project_v(pe, g + 1)
            pe.wait_ge(self.p_ready, g + 1)
            pe.wait_ge(self.v_taken, g + 1)
            if g:
                pe.wait_ge(self.o_taken, g)
            for h in range(2):
                pr = self.two(self.PR)[:, h, :]
                last = self.attend(pe, g, pr, lambda t: v[:, t * P + 64 * h:t * P + 64 * h + 64],
                                   k.bank[64 * h:64 * h + 64, 6, 0:S])
            last.then_inc(self.o_ready, 1)

    def act(self, act, chain):
        k, nc = self.k, self.k.nc

        def take_v(g):
            ready, count = self.v_projected(g)
            act.wait_ge(ready, count)
            if g >= 2:
                act.wait_ge(self.o_ready, g - 1)
            nc.scalar.activation(self.buf(self.V, g), k.bank[:, 1, 0:S], ACT.Copy).then_inc(self.v_taken, 1)

        take_v(0)
        for g in range(self.G):
            act.wait_ge(self.abs_ready, g + 1)
            if g:
                act.wait_ge(self.l1_ready, g)
            chain(nc.scalar.activation(self.two(self.E), self.two(self.ABS), ACT.Exp, scale=-1.0))
            chain(nc.scalar.activation(self.two(self.E), self.two(self.E), ACT.Ln, bias=1.0), self.log_ready)
            if g + 1 < self.G:
                take_v(g + 1)
            act.wait_ge(self.logp_ready, g + 1)
            chain(nc.scalar.activation(self.two(self.ABS), self.two(self.ABS), ACT.Exp), self.expd)
            act.wait_ge(self.o_ready, g + 1)
            nc.scalar.activation(k.big[:, g, :], k.bank[:, 6, 0:S], ACT.Copy).then_inc(self.o_taken, 1)

    def dve(self, dve, chain):
        k, nc = self.k, self.k.nc

        def take_qk(g):
            dve.wait_ge(self.qk_ready, g + 1)
            if g >= 2:
                dve.wait_ge(self.z_ready, g - 1)
            nc.vector.tensor_scalar(self.buf(self.QT, g), k.bank[:, 0, 0:S], 0.125, None, ALU.mult)
            nc.vector.tensor_copy(self.buf(self.KT, g), k.bank[:, 0, S:2 * S]).then_inc(self.qk_taken, 1)

        take_qk(0)
        for g in range(self.G):
            z, suf = k.bank[:, 2:4, 0:TRI], k.bank[:, 4:6, 0:TRI]
            a, e, lb, l1, pr = (self.two(b) for b in (self.ABS, self.E, self.LB, self.L1, self.PR))
            mask = k.c("mask_lt").rearrange("p (a n) -> p a n", a=1).to_broadcast([P, 2, TRI])
            dve.wait_ge(self.z_ready, g + 1)
            chain(nc.vector.tensor_scalar(lb, z, -1.0, None, ALU.mult))
            chain(nc.vector.tensor_tensor(a, z, lb, ALU.max), self.abs_ready)
            dve.wait_ge(self.log_ready, g + 1)
            chain(nc.vector.scalar_tensor_tensor(lb, z, 0.0, e, ALU.min, ALU.subtract))
            chain(nc.vector.tensor_tensor(l1, lb, z, ALU.subtract))
            chain(nc.vector.tensor_tensor(l1, l1, mask, ALU.mult), self.l1_ready)
            if g + 1 < self.G:
                take_qk(g + 1)
            dve.wait_ge(self.suf_ready, g + 1)
            chain(nc.vector.tensor_tensor(a, lb, suf, ALU.add), self.logp_ready)
            dve.wait_ge(self.expd, g + 1)
            if g:
                dve.wait_ge(self.o_ready, g)
            chain(nc.vector.tensor_tensor(pr, a, mask, ALU.mult), self.p_ready)


class Softmax(Heads):
    COMP = 1
    QK, V, RAW, T1, SC, EX, W, PT = 0, 1024, 1536, 2048, 2560, 3328, 4096, 4480
    SCALE = 1.0
    OUT = 0

    TOTAL = dict.fromkeys(("qk_ready", "qk_taken", "v_taken", "rot_ready", "rope_done", "s_ready", "max_ready", "exp_ready",
                           "w_ready", "wt_ready", "pt_ready", "o_ready", "o_taken"), Heads.G)

    def name_sems(self, sem):
        self.qk_ready = sem("qk_ready")
        self.qk_taken = sem("qk_taken")
        self.v_taken = sem("v_taken")
        self.rot_ready = sem("rot_ready")
        self.rope_done = sem("rope_done")
        self.s_ready = sem("s_ready")
        self.max_ready = sem("max_ready")
        self.exp_ready = sem("exp_ready")
        self.w_ready = sem("w_ready")
        self.wt_ready = sem("wt_ready")
        self.pt_ready = sem("pt_ready")
        self.o_ready = sem("o_ready")
        self.o_taken = sem("o_taken")

    def qk(self, g):
        a = self.QK + (g % 2) * 2 * S
        return self.k.wk[:, a:a + 2 * S]

    def vbuf(self, g):
        a = self.V + (g % 2) * S
        return self.k.wk[:, a:a + S]

    def packed(self, base, n=0):
        return self.k.wk[:, base + n * TRI:base + (n + 1) * TRI]

    def weigh(self, pe, g):
        k, nc = self.k, self.k.nc
        w, pt, v = self.packed(self.W), self.packed(self.PT), self.vbuf(g)
        pe.wait_ge(self.w_ready, self.at(self.w_ready, g + 1))
        if g:
            pe.wait_ge(self.pt_ready, self.at(self.pt_ready, g))
        for n in range(3):
            last = nc.tensor.transpose(k.bank[:, 5, n * P:(n + 1) * P], w[:, n * P:(n + 1) * P], k.c("ident"))
        last.then_inc(self.wt_ready, 1)
        pe.wait_ge(self.pt_ready, self.at(self.pt_ready, g + 1))
        pe.wait_ge(self.v_taken, self.at(self.v_taken, g + 1))
        if g:
            pe.wait_ge(self.o_taken, self.at(self.o_taken, g))
        self.attend(pe, g, pt, lambda t: v[:, t * P:(t + 1) * P], k.bank[:, 6, 0:S]).then_inc(self.o_ready, 1)

    def take_v(self, act, g):
        ready, count = self.v_projected(g)
        act.wait_ge(ready, count)
        if g >= 2:
            act.wait_ge(self.o_ready, self.at(self.o_ready, g - 1))
        self.k.nc.scalar.activation(self.vbuf(g), self.k.bank[:, 1, 0:S], ACT.Copy).then_inc(self.v_taken, 1)

    def soft_act(self, act, g):
        k, nc = self.k, self.k.nc
        act.wait_ge(self.max_ready, self.at(self.max_ready, g + 1))
        for n in range(self.COMP):
            for q, cols in ((0, slice(0, P)), (1, slice(P, TRI))):
                last = nc.scalar.activation(self.packed(self.EX, n)[:, cols], self.packed(self.SC, n)[:, cols], ACT.Exp,
                                            bias=k.ss[:, 2 * n + q:2 * n + q + 1],
                                            accum_out=k.ss[:, 4 + 2 * n + q:5 + 2 * n + q])
        last.then_inc(self.exp_ready, 1)

    def out_act(self, act, g):
        k, nc = self.k, self.k.nc
        act.wait_ge(self.wt_ready, self.at(self.wt_ready, g + 1))
        if g:
            act.wait_ge(self.o_ready, self.at(self.o_ready, g))
        nc.scalar.activation(self.packed(self.PT), k.bank[:, 5, 0:TRI], ACT.Copy).then_inc(self.pt_ready, 1)
        act.wait_ge(self.o_ready, self.at(self.o_ready, g + 1))
        nc.scalar.activation(k.big[:, self.OUT + g, :], k.bank[:, 6, 0:S], ACT.Copy).then_inc(self.o_taken, 1)

    def soft_max(self, dve, g, chain):
        k, nc = self.k, self.k.nc
        dve.wait_ge(self.s_ready, self.at(self.s_ready, g + 1))
        for n in range(self.COMP):
            sc = self.packed(self.SC, n)
            chain(nc.vector.scalar_tensor_tensor(sc, k.bank[:, 3 + n, 0:TRI], self.SCALE, k.c("causal_add"),
                                                 ALU.mult, ALU.add))
            for q, cols in ((0, slice(0, P)), (1, slice(P, TRI))):
                last = nc.vector.tensor_reduce(k.ss[:, 2 * n + q:2 * n + q + 1], sc[:, cols], AX, ALU.max, negate=True)
        chain(last, self.max_ready)

    def soft_div(self, dve, g, chain):
        k, nc = self.k, self.k.nc
        dve.wait_ge(self.exp_ready, self.at(self.exp_ready, g + 1))
        if g:
            dve.wait_ge(self.wt_ready, self.at(self.wt_ready, g))
        n = 2 * self.COMP
        chain(nc.vector.reciprocal(k.ss[:, 8:8 + n], k.ss[:, 4:4 + n]))
        if self.COMP == 2:
            chain(nc.vector.tensor_scalar(k.ss[:, 10:12], k.ss[:, 10:12], k.ss[:, 15:16], None, ALU.mult))
        w = self.packed(self.W)
        for q, cols in ((0, slice(0, P)), (1, slice(P, TRI))):
            last = nc.vector.tensor_scalar(w[:, cols], self.packed(self.EX)[:, cols], k.ss[:, 8 + q:9 + q], None, ALU.mult)
        if self.COMP == 2:
            chain(last)
            for q, cols in ((0, slice(0, P)), (1, slice(P, TRI))):
                last = nc.vector.scalar_tensor_tensor(w[:, cols], self.packed(self.EX, 1)[:, cols],
                                                      k.ss[:, 10 + q:11 + q], w[:, cols], ALU.mult, ALU.add)
        chain(last, self.w_ready)


class Roped(Softmax):

    def __init__(self, k, name, w, q0, k0, v0, comp, scale, rot, cos, sin, out):
        super().__init__(k, name, w, q0, k0, v0)
        self.COMP, self.SCALE, self.rot, self.cos, self.sin, self.OUT = comp, scale, rot, cos, sin, out

    def pe(self, pe):
        k, nc = self.k, self.k.nc

        def rotate(g):
            pe.wait_ge(self.qk_taken, self.at(self.qk_taken, g + 1))
            if g:
                pe.wait_ge(self.rope_done, self.at(self.rope_done, g))
            nc.tensor.matmul(k.bank[:, 2, :], k.c(self.rot), k.wk[:, self.RAW:self.RAW + 2 * S],
                             start=True, stop=True).then_inc(self.rot_ready, 1)

        self.project_qk(pe, 0)
        self.project_v(pe, 0)
        rotate(0)
        for g in range(self.G):
            pe.wait_ge(self.rope_done, self.at(self.rope_done, g + 1))
            if g:
                pe.wait_ge(self.max_ready, self.at(self.max_ready, g))
            d = P // self.COMP
            for n in range(self.COMP):
                q, kk = self.qk(g)[n * d:(n + 1) * d, 0:S], self.qk(g)[n * d:(n + 1) * d, S:2 * S]
                nc.tensor.matmul(k.bank[:, 3 + n, 0:P], q[:, 0:P], kk[:, 0:P], start=True, stop=True)
                last = nc.tensor.matmul(k.bank[:, 3 + n, P:TRI], q[:, P:S], kk, start=True, stop=True)
            last.then_inc(self.s_ready, 1)
            if g + 1 < self.G:
                self.project_qk(pe, g + 1)
                self.project_v(pe, g + 1)
                rotate(g + 1)
            self.weigh(pe, g)

    def act(self, act, chain):
        k, nc = self.k, self.k.nc

        def take(g):
            act.wait_ge(self.qk_ready, self.at(self.qk_ready, g + 1))
            if g:
                act.wait_ge(self.rope_done, self.at(self.rope_done, g))
            nc.scalar.activation(k.wk[:, self.RAW:self.RAW + 2 * S], k.bank[:, 0, :], ACT.Copy).then_inc(self.qk_taken, 1)
            self.take_v(act, g)

        take(0)
        for g in range(self.G):
            self.soft_act(act, g)
            if g + 1 < self.G:
                take(g + 1)
            self.out_act(act, g)

    def dve(self, dve, chain):
        k, nc = self.k, self.k.nc

        def two(ap):
            return ap.rearrange("p (a n) -> p a n", a=2)

        def rope(g):
            dve.wait_ge(self.qk_taken, self.at(self.qk_taken, g + 1))
            if g >= 2:
                dve.wait_ge(self.s_ready, self.at(self.s_ready, g - 1))
            raw, t1 = two(k.wk[:, self.RAW:self.RAW + 2 * S]), two(k.wk[:, self.T1:self.T1 + 2 * S])
            out = two(self.qk(g))
            cos, sin = (self.angle(x).rearrange("p (a n) -> p a n", a=1).to_broadcast([P, 2, S]) for x in (self.cos, self.sin))
            chain(nc.vector.tensor_tensor(t1, raw, cos, ALU.mult))
            dve.wait_ge(self.rot_ready, self.at(self.rot_ready, g + 1))
            chain(nc.vector.tensor_tensor(out, two(k.bank[:, 2, :]), sin, ALU.mult))
            chain(nc.vector.tensor_tensor(out, out, t1, ALU.add), self.rope_done)

        rope(0)
        for g in range(self.G):
            self.soft_max(dve, g, chain)
            self.soft_div(dve, g, chain)
            if g + 1 < self.G:
                rope(g + 1)

    def angle(self, name):
        return name if not isinstance(name, str) else self.k.c(name)


class Latent(Stage):
    UNITS = 2
    NQ, NKV = 3, 2

    def name_sems(self, sem):
        self.up_ready = sem("up_ready")
        self.taken = sem("taken")
        self.squared = sem("squared")
        self.sum_ready = sem("sum_ready")
        self.var_ready = sem("var_ready")
        self.root_ready = sem("root_ready")
        self.rot_ready = sem("rot_ready")

    def sp(self, sp):
        w = self.k.arg["w_in_2"][0]
        parts = [(self.k.slot(self.slot_of(0), 0, KC, 512), rows_of(w, 0, 512))]
        sp.wait_ge(self.k.w_used, self.freed(0))
        for dst, src in parts:
            sp.dma_start(dst, src).then_inc(self.loaded(0), UNIT_INC // len(parts))
        parts = [(self.k.slot(self.slot_of(1), 0, KC, 192), rows_of(w, 512, 192))]
        sp.wait_ge(self.k.w_used, self.freed(1))
        for dst, src in parts:
            sp.dma_start(dst, src).then_inc(self.loaded(1), UNIT_INC // len(parts))

    def lat(self, c):
        return self.k.wk[:, c * S:(c + 1) * S]

    def pe(self, pe):
        k, nc = self.k, self.k.nc
        for c in range(6):
            j, m = c // 4, (64 if c == 5 else P)
            if c % 4 == 0:
                pe.wait_ge(self.loaded(j), self.loads(j))
            w = k.slot(self.slot_of(j), 0, KC, 512 if j == 0 else 192)
            for q in range(KC):
                last = nc.tensor.matmul(k.bank[0:m, c // 2, (c % 2) * S:(c % 2 + 1) * S], w[:, q, (c % 4) * P:(c % 4) * P + m],
                                        k.hT[:, q, :], start=q == 0, stop=q == KC - 1)
            if c % 2:
                last.then_inc(self.up_ready if c == 1 else k.w_used, 1)
        pe.wait_ge(self.taken, 4)
        nc.tensor.matmul(k.bank[0:64, 4, 0:S], k.c("rot64")[0:64, 0:64], self.lat(5)[0:64, :],
                         start=True, stop=True).then_inc(self.rot_ready, 1)
        pe.wait_ge(self.squared, 1)
        for a, n, o in ((0, self.NQ, 0), (self.NQ, self.NKV, S)):
            for c in range(n):
                last = nc.tensor.matmul(k.bank[:, 3, o:o + S], k.c("ones"), k.wk[:, 2048 + (a + c) * S:2048 + (a + c + 1) * S],
                                        start=c == 0, stop=c == n - 1)
        last.then_inc(self.sum_ready, 1)

    def act(self, act, chain):
        k, nc = self.k, self.k.nc
        for b in range(2):
            if b:
                act.wait_ge(self.k.w_used, self.used(0))
            else:
                act.wait_ge(self.up_ready, 1)
            chain(nc.scalar.activation(k.wk[:, 2 * b * S:(2 * b + 2) * S], k.bank[:, b, :], ACT.Copy), self.taken)
        act.wait_ge(self.k.w_used, self.used(1))
        chain(nc.scalar.activation(self.lat(4), k.bank[:, 2, 0:S], ACT.Copy), self.taken)
        chain(nc.scalar.activation(self.lat(5)[0:64, :], k.bank[0:64, 2, S:2 * S], ACT.Copy), self.taken)
        chain(nc.scalar.activation(k.wk[:, 2048:2048 + 5 * S], k.wk[:, 0:5 * S], ACT.Square), self.squared)
        act.wait_ge(self.var_ready, 1)
        chain(nc.scalar.activation(k.wk[:, 4096:4096 + 2 * S], k.wk[:, 4096:4096 + 2 * S], ACT.Sqrt), self.root_ready)

    def dve(self, dve, chain):
        k, nc = self.k, self.k.nc
        dve.wait_ge(self.rot_ready, 1)
        t1 = k.wk[0:64, 5120:5120 + S]
        chain(nc.vector.tensor_tensor(t1, self.lat(5)[0:64, :], k.c("cos64")[0:64, :], ALU.mult))
        chain(nc.vector.tensor_tensor(k.big[0:64, 21, :], k.bank[0:64, 4, 0:S], k.c("sin64")[0:64, :], ALU.mult))
        chain(nc.vector.tensor_tensor(k.big[0:64, 21, :], k.big[0:64, 21, :], t1, ALU.add))
        dve.wait_ge(self.sum_ready, 1)
        for n, o in ((self.NQ, 0), (self.NKV, S)):
            chain(nc.vector.tensor_scalar(k.wk[:, 4096 + o:4096 + o + S], k.bank[:, 3, o:o + S], 1.0 / (n * P), EPS6,
                                          ALU.mult, ALU.add), self.var_ready if o else None)
        dve.wait_ge(self.root_ready, 1)
        inv = k.wk[:, 4608:4608 + 2 * S]
        chain(nc.vector.reciprocal(inv, k.wk[:, 4096:4096 + 2 * S]))
        for c in range(5):
            gain = k.p("q_norm_2", c) if c < self.NQ else k.p("kv_norm_2", c - self.NQ)
            o = 0 if c < self.NQ else S
            nc.vector.scalar_tensor_tensor(k.big[:, 16 + c, :], self.lat(c), gain, inv[:, o:o + S], ALU.mult, ALU.mult)


class Mla(Softmax):
    UNITS = 4
    SCALE = 192.0 ** -0.5
    OUT = 0
    QR = 5000

    def name_sems(self, sem):
        super().name_sems(sem)
        self.v_ready = sem("v_ready")

    def __init__(self, k, name):
        Stage.__init__(self, k, name)

    def sp(self, sp):
        for j in range(self.UNITS):
            s = self.slot_of(j)
            parts = [(self.k.slot(s, 0, 3, 384), rows_of(self.k.arg["w_uq_2"][0], j * 384, 384)),
                              (self.k.slot(s, 1152, 2, 512), rows_of(self.k.arg["w_ukv_2"][0], j * 512, 512))]
            sp.wait_ge(self.k.w_used, self.freed(j))
            for dst, src in parts:
                sp.dma_start(dst, src).then_inc(self.loaded(j), UNIT_INC // len(parts))

    def v_projected(self, g):
        return self.v_ready, g + 1

    def qr(self, g):
        a = self.QR + (g % 2) * S
        return self.k.wk[0:64, a:a + S]

    def pe(self, pe):
        k, nc = self.k, self.k.nc
        qlat, kvlat = k.big[:, 16:19, :], k.big[:, 19:21, :]

        def project(g):
            j, h = g // 2, g % 2
            if h == 0:
                pe.wait_ge(self.loaded(j), self.loads(j))
            s = self.slot_of(j)
            uq, ukv = k.slot(s, 0, 3, 384), k.slot(s, 1152, 2, 512)
            if g:
                pe.wait_ge(self.qk_taken, g)
                pe.wait_ge(self.rope_done, g)
                pe.wait_ge(self.v_taken, g)
            for t in range(T):
                for c in range(2):
                    last = nc.tensor.matmul(k.bank[:, 1, t * P:(t + 1) * P], kvlat[:, c, t * P:(t + 1) * P],
                                            ukv[:, c, h * 256 + P:(h + 1) * 256], start=c == 0, stop=c == 1)
            last.then_inc(self.v_ready, 1)
            for c in range(3):
                nc.tensor.matmul(k.bank[:, 0, 0:S], uq[:, c, h * 192:h * 192 + P], qlat[:, c, :], start=c == 0, stop=c == 2)
            for c in range(2):
                nc.tensor.matmul(k.bank[:, 0, S:2 * S], ukv[:, c, h * 256:h * 256 + P], kvlat[:, c, :], start=c == 0, stop=c == 1)
            for c in range(3):
                last = nc.tensor.matmul(k.bank[0:64, 2, 0:S], uq[:, c, h * 192 + P:(h + 1) * 192], qlat[:, c, :],
                                        start=c == 0, stop=c == 2)
            last.then_inc(self.qk_ready, 1)
            pe.wait_ge(self.qk_taken, g + 1)
            nc.tensor.matmul(k.bank[0:64, 2, S:2 * S], k.c("rot64")[0:64, 0:64], k.wk[0:64, self.RAW:self.RAW + S],
                             start=True, stop=True).then_inc(self.rot_ready, 1)

        project(0)
        for g in range(self.G):
            pe.wait_ge(self.rope_done, g + 1)
            if g:
                pe.wait_ge(self.max_ready, g)
            q, kn, qr, kr = self.qk(g)[:, 0:S], self.qk(g)[:, S:2 * S], self.qr(g), k.big[0:64, 21, :]
            for cols, qs, n in ((slice(0, P), slice(0, P), P), (slice(P, TRI), slice(P, S), S)):
                first = nc.tensor.matmul(k.bank[:, 3, cols], q[:, qs], kn[:, 0:n], start=True, stop=False)
                if g % 2 and n == P:
                    first.then_inc(k.w_used, 1)
                last = nc.tensor.matmul(k.bank[:, 3, cols], qr[:, qs], kr[:, 0:n], start=False, stop=True)
            last.then_inc(self.s_ready, 1)
            if g + 1 < self.G:
                project(g + 1)
            self.weigh(pe, g)

    def act(self, act, chain):
        k, nc = self.k, self.k.nc

        def take(g):
            act.wait_ge(self.qk_ready, g + 1)
            if g >= 2:
                act.wait_ge(self.s_ready, g - 1)
            if g:
                act.wait_ge(self.rope_done, g)
            nc.scalar.activation(self.qk(g), k.bank[:, 0, :], ACT.Copy)
            nc.scalar.activation(k.wk[0:64, self.RAW:self.RAW + S], k.bank[0:64, 2, 0:S], ACT.Copy).then_inc(self.qk_taken, 1)
            self.take_v(act, g)

        take(0)
        for g in range(self.G):
            self.soft_act(act, g)
            if g + 1 < self.G:
                take(g + 1)
            self.out_act(act, g)

    def dve(self, dve, chain):
        k, nc = self.k, self.k.nc

        def rope(g):
            dve.wait_ge(self.rot_ready, g + 1)
            if g >= 2:
                dve.wait_ge(self.s_ready, g - 1)
            t1 = k.wk[0:64, self.T1:self.T1 + S]
            chain(nc.vector.tensor_tensor(t1, k.wk[0:64, self.RAW:self.RAW + S], k.c("cos64")[0:64, :], ALU.mult))
            chain(nc.vector.tensor_tensor(self.qr(g), k.bank[0:64, 2, S:2 * S], k.c("sin64")[0:64, :], ALU.mult))
            chain(nc.vector.tensor_tensor(self.qr(g), self.qr(g), t1, ALU.add), self.rope_done)

        rope(0)
        for g in range(self.G):
            self.soft_max(dve, g, chain)
            self.soft_div(dve, g, chain)
            if g + 1 < self.G:
                rope(g + 1)


class Merge(Stage):
    TOTAL = {"gate_ready": 2 * KC, "merged": KC}

    def name_sems(self, sem):
        self.gate_ready = sem("gate_ready")
        self.merged = sem("merged")

    def __init__(self, k, name, ya, wa, yb, wb, w_in, ga, gb, bias):
        self.per = 1 if yb.shape[1] == KC else 2
        self.UNITS = KC * self.per
        super().__init__(k, name)
        self.ya, self.wa, self.yb, self.wb, self.w_in, self.ga, self.gb, self.bias = ya, wa, yb, wb, w_in, ga, gb, bias

    def parts(self, c):
        a, ga, gb = (0, self.ya, self.wa, c * P), (2, self.k.hT, self.w_in, self.ga + c * P), (3, self.k.hT, self.w_in, self.gb + c * P)
        b = (1, self.yb, self.wb, c * P)
        return [[a, b, ga, gb]] if self.per == 1 else [[a, ga, gb], [b]]

    def view(self, j, n, chunks):
        return self.k.slot(self.slot_of(j), n * KC * P, chunks, P)

    def sp(self, sp):
        for c in range(KC):
            for u, parts in enumerate(self.parts(c)):
                j = c * self.per + u
                parts = [(self.view(j, n, src.shape[1]), rows_of(w, col, P)) for n, (_, src, w, col) in enumerate(parts)]
                sp.wait_ge(self.k.w_used, self.freed(j))
                for dst, src in parts:
                    sp.dma_start(dst, src).then_inc(self.loaded(j), UNIT_INC // len(parts))

    def pe(self, pe):
        k, nc = self.k, self.k.nc
        for c in range(KC):
            if c >= 2:
                pe.wait_ge(self.merged, self.at(self.merged, c - 1))
            for u, parts in enumerate(self.parts(c)):
                j = c * self.per + u
                pe.wait_ge(self.loaded(j), self.loads(j))
                for n, (half, src, w, col) in enumerate(parts):
                    v, chunks = self.view(j, n, src.shape[1]), src.shape[1]
                    out = k.bank[:, 2 * (c % 2) + half // 2, (half % 2) * S:(half % 2 + 1) * S]
                    for q in range(chunks):
                        last = nc.tensor.matmul(out, v[:, q, :], src[:, q, :], start=q == 0, stop=q == chunks - 1)
                last.then_inc(k.w_used, 1)

    def act(self, act, chain):
        k, nc = self.k, self.k.nc
        for c in range(KC):
            act.wait_ge(self.k.w_used, self.used((c + 1) * self.per - 1))
            if c >= 2:
                act.wait_ge(self.merged, self.at(self.merged, c - 1))
            for h in range(2):
                kw = {"bias": k.p(self.bias, h * KC + c)} if self.bias else {}
                nc.scalar.activation(k.wk[:, 2048 + (2 * (c % 2) + h) * S:2048 + (2 * (c % 2) + h + 1) * S],
                                     k.bank[:, 2 * (c % 2) + 1, h * S:(h + 1) * S], ACT.Sigmoid, **kw).then_inc(self.gate_ready, 1)

    def dve(self, dve, chain):
        k, nc = self.k, self.k.nc
        for c in range(KC):
            dve.wait_ge(self.gate_ready, self.at(self.gate_ready, 2 * c + 2))
            both = k.wk[:, 2048 + 2 * (c % 2) * S:2048 + 2 * (c % 2 + 1) * S]
            chain(nc.vector.tensor_tensor(k.wk[:, 3072:3072 + 2 * S], k.bank[:, 2 * (c % 2), :], both, ALU.mult))
            chain(nc.vector.tensor_tensor(k.wk[:, c * S:(c + 1) * S], k.wk[:, 3072:3072 + S], k.wk[:, 3072 + S:3072 + 2 * S],
                                          ALU.add), self.merged)


class Angles(Stage):
    MAGIC = 12582912.0
    TWO_PI = (6.28125, 0.0019350051879882812, 3.0199157663e-07)

    def name_sems(self, sem):
        self.pos_loaded = sem("pos_loaded")
        self.reduced = sem("reduced")
        self.sin_ready = sem("sin_ready")
        self.dots = sem("dots")
        self.lam_exp = sem("lam_exp")

    def act(self, act, chain):
        k, nc = self.k, self.k.nc
        act.dma_start(k.pos[:, :], k.arg["positions_3"].to_broadcast([P, S])).then_inc(self.pos_loaded, 16)
        act.wait_ge(self.dots, 1)
        chain(nc.scalar.activation(k.ss[:, 12:14], k.ss[:, 12:14], ACT.Exp), self.lam_exp)
        act.wait_ge(self.reduced, 1)
        chain(nc.scalar.activation(k.wk[:, 8192:8192 + 2 * S], k.wk[:, 8192:8192 + 2 * S], ACT.Sin), self.sin_ready)

    def dve(self, dve, chain):
        k, nc = self.k, self.k.nc
        for n, (a, b) in enumerate((("lambda_q1_3", "lambda_k1_3"), ("lambda_q2_3", "lambda_k2_3"))):
            chain(nc.vector.tensor_tensor(k.wk[:, n * 64:(n + 1) * 64], k.r(a), k.r(b), ALU.mult))
            chain(nc.vector.tensor_reduce(k.ss[:, 12 + n:13 + n], k.wk[:, n * 64:(n + 1) * 64], AX, ALU.add),
                  self.dots if n else None)
        dve.wait_ge(self.lam_exp, 1)
        chain(nc.vector.tensor_tensor(k.ss[:, 15:16], k.ss[:, 13:14], k.ss[:, 12:13], ALU.subtract))
        chain(nc.vector.tensor_scalar(k.ss[:, 15:16], k.ss[:, 15:16], -0.2, None, ALU.add))
        dve.wait_ge(self.pos_loaded, 16)
        ang, n, r, c = (k.wk[:, 512 + m * S:512 + (m + 1) * S] for m in range(4))
        cos, sin = k.wk[:, 8192:8192 + S], k.wk[:, 8192 + S:8192 + 2 * S]
        chain(nc.vector.tensor_copy(r, k.pos[:, :]))
        chain(nc.vector.tensor_scalar(ang, r, k.c("inv_freq"), None, ALU.mult))
        chain(nc.vector.tensor_scalar(n, ang, float(1.0 / (2.0 * np.pi)), self.MAGIC, ALU.mult, ALU.add))
        chain(nc.vector.tensor_scalar(n, n, self.MAGIC, None, ALU.subtract))
        src = ang
        for part in self.TWO_PI:
            chain(nc.vector.scalar_tensor_tensor(r, n, -part, src, ALU.mult, ALU.add))
            src = r
        pi = float(np.nextafter(np.float32(np.pi), np.float32(0)))
        chain(nc.vector.tensor_scalar(sin, r, pi, -pi, ALU.min, ALU.max))
        chain(nc.vector.tensor_scalar(r, r, float(np.pi / 2), None, ALU.add))
        chain(nc.vector.tensor_scalar(c, r, float(np.pi), float(-2 * np.pi), ALU.is_gt, ALU.mult))
        chain(nc.vector.tensor_tensor(r, r, c, ALU.add))
        chain(nc.vector.tensor_scalar(cos, r, pi, -pi, ALU.min, ALU.max), self.reduced)


class SubNorm(Stage):

    def name_sems(self, sem):
        self.squared = sem("squared")
        self.sum_ready = sem("sum_ready")
        self.var_ready = sem("var_ready")
        self.root_ready = sem("root_ready")

    def act(self, act, chain):
        k, nc = self.k, self.k.nc
        chain(nc.scalar.activation(k.big[:, 0:8, :], k.big[:, 16:24, :], ACT.Square), self.squared)
        act.wait_ge(self.var_ready, 1)
        chain(nc.scalar.activation(k.big[:, 0:8, :], k.big[:, 0:8, :], ACT.Sqrt), self.root_ready)

    def pe(self, pe):
        k, nc = self.k, self.k.nc
        pe.wait_ge(self.squared, 1)
        for b in range(4):
            last = nc.tensor.matmul(k.bank[:, b, :], k.c("ones"), k.big[:, 2 * b:2 * b + 2, :], start=True, stop=True)
        last.then_inc(self.sum_ready, 1)

    def dve(self, dve, chain):
        k, nc = self.k, self.k.nc
        dve.wait_ge(self.sum_ready, 1)
        chain(nc.vector.tensor_scalar(k.big[:, 0:8, :], k.bank[:, 0:4, :].rearrange("p a (b n) -> p (a b) n", b=2), 1.0 / P, EPS5,
                                      ALU.mult, ALU.add), self.var_ready)
        chain(nc.vector.tensor_scalar(k.ss[:, 14:15], k.p("subln_w_3", 0), 0.8, None, ALU.mult))
        dve.wait_ge(self.root_ready, 1)
        chain(nc.vector.reciprocal(k.big[:, 8:16, :], k.big[:, 0:8, :]))
        nc.vector.scalar_tensor_tensor(k.big[:, 16:24, :], k.big[:, 16:24, :], k.ss[:, 14:15], k.big[:, 8:16, :],
                                       ALU.mult, ALU.mult)


class StepSizes(Stage):
    UNITS = 1

    def name_sems(self, sem):
        self.abs_ready = sem("abs_ready")
        self.log_ready = sem("log_ready")
        self.da_ready = sem("da_ready")
        self.cum_ready = sem("cum_ready")
        self.tail_ready = sem("tail_ready")

    def sp(self, sp):
        parts = [(self.k.slot(self.slot_of(0), 0, KC, 32), rows_of(self.k.arg["w_in_3"][0], 9216, 32))]
        sp.wait_ge(self.k.w_used, self.freed(0))
        for dst, src in parts:
            sp.dma_start(dst, src).then_inc(self.loaded(0), UNIT_INC // len(parts))

    def pe(self, pe):
        k, nc = self.k, self.k.nc
        pe.wait_ge(self.loaded(0), self.loads(0))
        w = k.slot(self.slot_of(0), 0, KC, 32)
        for t in range(T):
            for c in range(KC):
                last = nc.tensor.matmul(k.bank[:, 0, t * 32:(t + 1) * 32], k.hT[:, c, t * P:(t + 1) * P], w[:, c, :],
                                        start=c == 0, stop=c == KC - 1)
        last.then_inc(k.w_used, 1)
        pe.wait_ge(self.da_ready, 1)
        nc.tensor.matmul(k.bank[:, 1, 0:64], k.c("le"), k.sd[:, 2:4, :], start=True, stop=True)
        nc.tensor.matmul(k.bank[:, 1, 64:96], k.c("ones"), k.sd[:, 2, :], start=True, stop=True).then_inc(self.cum_ready, 1)

    def act(self, act, chain):
        k, nc = self.k, self.k.nc
        chain(nc.scalar.activation(k.wk[:, 256:288], k.r("a_log_3"), ACT.Exp))
        act.wait_ge(self.abs_ready, 1)
        chain(nc.scalar.activation(k.wk[:, 128:192], k.wk[:, 64:128], ACT.Exp, scale=-1.0))
        chain(nc.scalar.activation(k.wk[:, 128:192], k.wk[:, 128:192], ACT.Ln, bias=1.0), self.log_ready)
        act.wait_ge(self.tail_ready, 1)
        chain(nc.scalar.activation(k.sd[:, 6:8, :], k.sd[:, 6:8, :], ACT.Exp))

    def dve(self, dve, chain):
        k, nc = self.k, self.k.nc

        def two(ap):
            return ap.rearrange("p (a n) -> p a n", a=2)
        v, a, log = two(k.wk[:, 0:64]), two(k.wk[:, 64:128]), two(k.wk[:, 128:192])
        bias = k.r("dt_bias_3").rearrange("p (a n) -> p a n", a=1).to_broadcast([P, T, 32])
        dve.wait_ge(self.k.w_used, self.used(0))
        chain(nc.vector.tensor_tensor(v, two(k.bank[:, 0, 0:64]), bias, ALU.add))
        chain(nc.vector.scalar_tensor_tensor(a, v, -1.0, v, ALU.mult, ALU.max), self.abs_ready)
        dve.wait_ge(self.log_ready, 1)
        chain(nc.vector.scalar_tensor_tensor(k.sd[:, 0:2, :], v, 0.0, log, ALU.max, ALU.add))
        ea = k.wk[:, 256:288].rearrange("p (a n) -> p a n", a=1).to_broadcast([P, T, 32])
        chain(nc.vector.scalar_tensor_tensor(k.sd[:, 2:4, :], k.sd[:, 0:2, :], -1.0, ea, ALU.mult, ALU.mult), self.da_ready)
        dve.wait_ge(self.cum_ready, 1)
        chain(nc.vector.tensor_copy(k.sd[:, 4:6, :], two(k.bank[:, 1, 0:64])))
        chain(nc.vector.tensor_tensor(k.sd[:, 6, :], k.bank[:, 1, 64:96], k.sd[:, 4, :], ALU.subtract))
        chain(nc.vector.tensor_copy(k.sd[:, 7, :], k.sd[:, 5, :]), self.tail_ready)


class Ssd(Stage):
    G, R, D = 8, 4, 64
    UNITS = 16
    PADW = S + 3
    PAD, CV, SV, SEG, XT, XDT, XW, CB, Y, ZS, TMP = 0, 1036, 2060, 3084, 4108, 4620, 5132, 5388, 5772, 6284, 6796

    def name_sems(self, sem):
        self.copied = sem("copied")
        self.conv_done = sem("conv_done")
        self.conv_silu = sem("conv_silu")
        self.z_silu = sem("z_silu")
        self.cum_bc = sem("cum_bc")
        self.seg_done = sem("seg_done")
        self.decay_ready = sem("decay_ready")
        self.turned = sem("turned")
        self.x_taken = sem("x_taken")
        self.m_ready = sem("m_ready")
        self.y_ready = sem("y_ready")
        self.y_summed = sem("y_summed")
        self.y_squared = sem("y_squared")
        self.var_ready = sem("var_ready")
        self.root_ready = sem("root_ready")
        self.y_scaled = sem("y_scaled")
        self.yt_ready = sem("yt_ready")
        self.yt_taken = sem("yt_taken")
        self.pads_zero = sem("pads_zero")

    def w4(self, base, n):
        return self.k.wk[:, base:base + n]

    def conv_chunk(self, g, n):
        return (2 * g, 2 * g + 1, 16 + g, 24 + g)[n]

    def sp(self, sp):
        w = self.k.arg["w_in_3"][0]
        for g in range(self.G):
            a, b = self.k.slot(self.slot_of(2 * g), 0, KC, 512), self.k.slot(self.slot_of(2 * g + 1), 0, KC, 256)
            parts = [(a[:, :, 0:256], rows_of(w, 5120 + g * 256, 256)),
                                  (a[:, :, 256:384], rows_of(w, 7168 + g * P, P)),
                                  (a[:, :, 384:512], rows_of(w, 8192 + g * P, P))]
            sp.wait_ge(self.k.w_used, self.freed(2 * g))
            for dst, src in parts:
                sp.dma_start(dst, src).then_inc(self.loaded(2 * g), UNIT_INC // len(parts))
            parts = [(b, rows_of(w, 3072 + g * 256, 256))]
            sp.wait_ge(self.k.w_used, self.freed(2 * g + 1))
            for dst, src in parts:
                sp.dma_start(dst, src).then_inc(self.loaded(2 * g + 1), UNIT_INC // len(parts))

    def pe(self, pe):
        k, nc = self.k, self.k.nc
        sv, cb = self.w4(self.SV, 1024), self.w4(self.CB, TRI)

        def project_x(g):
            pe.wait_ge(self.loaded(2 * g), self.loads(2 * g))
            w = k.slot(self.slot_of(2 * g), 0, KC, 512)
            if g:
                pe.wait_ge(self.copied, 2 * g)
            for n in range(4):
                for c in range(KC):
                    last = nc.tensor.matmul(k.bank[:, n // 2, (n % 2) * S:(n % 2 + 1) * S], w[:, c, n * P:(n + 1) * P],
                                            k.hT[:, c, :], start=c == 0, stop=c == KC - 1)
            last.then_inc(k.w_used, 1)

        def project_z(g):
            pe.wait_ge(self.loaded(2 * g + 1), self.loads(2 * g + 1))
            w = k.slot(self.slot_of(2 * g + 1), 0, KC, 256)
            if g:
                pe.wait_ge(self.z_silu, g)
            for t in range(T):
                for c in range(KC):
                    last = nc.tensor.matmul(k.bank[:, 2, t * S:(t + 1) * S], k.hT[:, c, t * P:(t + 1) * P], w[:, c, :],
                                            start=c == 0, stop=c == KC - 1)
            last.then_inc(k.w_used, 1)

        def turn_y(g):
            pe.wait_ge(self.y_scaled, g + 1)
            pe.wait_ge(self.m_ready, g + 1)
            for ch in range(2):
                for t in range(T):
                    last = nc.tensor.transpose(k.bank[:, 4, ch * S + t * P:ch * S + (t + 1) * P],
                                               self.w4(self.Y, 512)[:, t * S + ch * P:t * S + (ch + 1) * P], k.c("ident"))
            last.then_inc(self.yt_ready, 1)

        project_x(0)
        project_z(0)
        for g in range(self.G):
            if g:
                pe.wait_ge(self.seg_done, g)
            for c in range(T):
                for r in range(self.R):
                    last = nc.tensor.matmul(k.bank[:, 5 + c, r * P:(r + 1) * P],
                                            k.sd[:, 2 + c, 4 * g + r:4 * g + r + 1].to_broadcast([P, P]), k.c("le"),
                                            start=True, stop=True)
            last.then_inc(self.cum_bc, 1)
            if g:
                turn_y(g - 1)
            pe.wait_ge(self.conv_silu, g + 1)
            if g:
                pe.wait_ge(self.y_summed, g)
                pe.wait_ge(self.yt_taken, g)
            for t in range(T):
                for ch in range(2):
                    nc.tensor.transpose(k.bank[:, 3, t * S + ch * P:t * S + (ch + 1) * P],
                                        sv[:, ch * S + t * P:ch * S + (t + 1) * P], k.c("ident"))
            bt, ct = sv[:, 512:768], sv[:, 768:1024]
            nc.tensor.matmul(k.bank[:, 4, 0:S], bt[:, 0:P], ct, start=True, stop=True)
            nc.tensor.matmul(k.bank[:, 4, S:TRI], bt[:, P:S], ct[:, P:S], start=True, stop=True).then_inc(self.turned, 1)
            if g + 1 < self.G:
                project_x(g + 1)
            pe.wait_ge(self.m_ready, g + 1)
            pe.wait_ge(self.x_taken, g + 1)
            seg, xdt = self.w4(self.SEG, 1024), self.w4(self.XDT, 512)
            for c in range(T):
                for r in range(self.R):
                    nc.tensor.matmul(k.bank[:, 7, c * S + r * self.D:c * S + (r + 1) * self.D],
                                     seg[:, c * 512 + r * P:c * 512 + (r + 1) * P], xdt[:, c * S + r * self.D:c * S + (r + 1) * self.D],
                                     start=True, stop=True)
            nc.tensor.matmul(k.bank[:, 3, 0:S], cb[:, P:S], self.w4(self.XW, S), start=True, stop=True).then_inc(self.y_ready, 1)
            if g + 1 < self.G:
                project_z(g + 1)
        turn_y(self.G - 1)

    def act(self, act, chain):
        k, nc = self.k, self.k.nc
        pad = self.w4(self.PAD, 4 * self.PADW).rearrange("p (a n) -> p a n", a=4)

        def copy_in(g):
            act.wait_ge(self.k.w_used, self.used(2 * g))
            if g:
                act.wait_ge(self.conv_done, g)
            for b in range(2):
                nc.scalar.activation(pad[:, 2 * b:2 * b + 2, 3:], k.bank[:, b, :].rearrange("p (a n) -> p a n", a=2),
                                     ACT.Copy).then_inc(self.copied, 1)

        def silu_z(g):
            act.wait_ge(self.k.w_used, self.used(2 * g + 1))
            if g:
                act.wait_ge(self.y_summed, g)
            nc.scalar.activation(self.w4(self.ZS, 512), k.bank[:, 2, :], ACT.Silu).then_inc(self.z_silu, 1)

        def silu_x(g):
            act.wait_ge(self.conv_done, g + 1)
            if g:
                act.wait_ge(self.turned, g)
            nc.scalar.activation(self.w4(self.SV, 1024), self.w4(self.CV, 1024), ACT.Silu).then_inc(self.conv_silu, 1)

        act.wait_ge(self.pads_zero, 1)
        copy_in(0)
        silu_x(0)
        silu_z(0)
        for g in range(self.G):
            act.wait_ge(self.seg_done, g + 1)
            chain(nc.scalar.activation(self.w4(self.SEG, 1024), self.w4(self.SEG, 1024), ACT.Exp), self.decay_ready)
            act.wait_ge(self.turned, g + 1)
            if g:
                act.wait_ge(self.y_summed, g)
            chain(nc.scalar.activation(self.w4(self.XT, 512), k.bank[:, 3, :], ACT.Copy), self.x_taken)
            if g + 1 < self.G:
                copy_in(g + 1)
                silu_x(g + 1)
            act.wait_ge(self.y_summed, g + 1)
            for t in range(T):
                last = nc.scalar.activation(self.w4(self.TMP, 512)[:, t * S:(t + 1) * S], self.w4(self.Y, 512)[:, t * S:(t + 1) * S],
                                            ACT.Square, accum_out=k.ss[:, t:t + 1])
            chain(last, self.y_squared)
            act.wait_ge(self.var_ready, g + 1)
            chain(nc.scalar.activation(k.ss[:, 4:6], k.ss[:, 2:4], ACT.Sqrt), self.root_ready)
            if g + 1 < self.G:
                silu_z(g + 1)
            act.wait_ge(self.yt_ready, g + 1)
            for ch in range(2):
                last = nc.scalar.activation(k.big[:, 2 * g + ch, :], k.bank[:, 4, ch * S:(ch + 1) * S], ACT.Copy,
                                            scale=k.p("ssd_norm_w_3", 2 * g + ch))
            last.then_inc(self.yt_taken, 1)

    def dve(self, dve, chain):
        k, nc = self.k, self.k.nc
        pad = self.w4(self.PAD, 4 * self.PADW).rearrange("p (a n) -> p a n", a=4)
        chain(nc.vector.memset(pad[:, :, 0:3], 0.0), self.pads_zero)

        def conv(g):
            dve.wait_ge(self.copied, 2 * g + 2)
            if g:
                dve.wait_ge(self.conv_silu, g)
            for j in (3, 2, 1, 0):
                for n in range(4):
                    c, acc = self.conv_chunk(g, n), self.w4(self.CV + n * S, S)
                    w = k.p("conv_w_3", j * 32 + c)
                    if j == 3:
                        last = nc.vector.tensor_scalar(acc, pad[:, n, j:j + S], w, k.p("conv_b_3", c), ALU.mult, ALU.add)
                    else:
                        last = nc.vector.scalar_tensor_tensor(acc, pad[:, n, j:j + S], w, acc, ALU.mult, ALU.add)
                    if n == 3:
                        chain(last, self.conv_done if j == 0 else None)

        def heads(ap, t=T):
            return ap.rearrange("p (t r d) -> p t r d", t=t, r=self.R)

        def per_head(cols, g, t=T):
            return k.sd[:, cols, 4 * g:4 * g + 4].rearrange("p t (r d) -> p t r d", d=1).to_broadcast([P, t, self.R, self.D])

        conv(0)
        for g in range(self.G):
            seg = self.w4(self.SEG, 1024)
            dve.wait_ge(self.cum_bc, g + 1)
            if g:
                dve.wait_ge(self.y_ready, g)
            for c in range(T):
                for r in range(self.R):
                    last = nc.vector.tensor_scalar(seg[:, c * 512 + r * P:c * 512 + (r + 1) * P], k.bank[:, 5 + c, r * P:(r + 1) * P],
                                                   k.sd[:, 4 + c, 4 * g + r:4 * g + r + 1], 0.0, ALU.subtract, ALU.min)
            chain(last, self.seg_done)
            dve.wait_ge(self.x_taken, g + 1)
            xt, xdt, xw = self.w4(self.XT, 512), self.w4(self.XDT, 512), self.w4(self.XW, S)
            chain(nc.vector.tensor_tensor(heads(xdt), heads(xt), per_head(slice(0, 2), g), ALU.mult))
            chain(nc.vector.tensor_tensor(heads(xw, 1), heads(xdt[:, 0:S], 1), per_head(slice(6, 7), g, 1), ALU.mult))
            cb = self.w4(self.CB, TRI)
            chain(nc.vector.tensor_tensor(cb, k.bank[:, 4, 0:TRI], k.c("mask_le"), ALU.mult))
            dve.wait_ge(self.decay_ready, g + 1)
            for c in range(T):
                m = seg[:, c * 512:(c + 1) * 512].rearrange("p (r n) -> p r n", r=self.R)
                last = nc.vector.tensor_tensor(m, m, cb[:, c * S:c * S + P].rearrange("p (r n) -> p r n", r=1)
                                               .to_broadcast([P, self.R, P]), ALU.mult)
            chain(last, self.m_ready)
            if g + 1 < self.G:
                conv(g + 1)
            y, tmp = self.w4(self.Y, 512), self.w4(self.TMP + 512, 512)
            skip = k.r("d_skip_3")[:, 4 * g:4 * g + 4].rearrange("p (t r d) -> p t r d", t=1, d=1).to_broadcast([P, T, self.R, self.D])
            chain(nc.vector.tensor_tensor(heads(tmp), heads(xt), skip, ALU.mult))
            dve.wait_ge(self.y_ready, g + 1)
            if g:
                dve.wait_ge(self.yt_ready, g)
            chain(nc.vector.tensor_tensor(y, k.bank[:, 7, :], tmp, ALU.add))
            chain(nc.vector.tensor_tensor(heads(tmp[:, 0:S], 1), heads(k.bank[:, 3, 0:S], 1), per_head(slice(7, 8), g, 1), ALU.mult))
            chain(nc.vector.tensor_tensor(y[:, S:], y[:, S:], tmp[:, 0:S], ALU.add))
            dve.wait_ge(self.z_silu, g + 1)
            chain(nc.vector.tensor_tensor(y, y, self.w4(self.ZS, 512), ALU.mult), self.y_summed)
            dve.wait_ge(self.y_squared, g + 1)
            chain(nc.vector.tensor_scalar(k.ss[:, 2:4], k.ss[:, 0:2], 1.0 / 256, EPS5, ALU.mult, ALU.add), self.var_ready)
            dve.wait_ge(self.root_ready, g + 1)
            chain(nc.vector.reciprocal(k.ss[:, 6:8], k.ss[:, 4:6]))
            for t in range(T):
                last = nc.vector.tensor_scalar(y[:, t * S:(t + 1) * S], y[:, t * S:(t + 1) * S], k.ss[:, 6 + t:7 + t], None, ALU.mult)
            chain(last, self.y_scaled)


class Route(Stage):
    UNITS = 1

    def name_sems(self, sem):
        self.oh_ready = sem("oh_ready")
        self.rank_ready = sem("rank_ready")
        self.dest_ready = sem("dest_ready")
        self.row_ready = sem("row_ready")
        self.exp_in = sem("exp_in")
        self.exp_out = sem("exp_out")
        self.rows_taken = sem("rows_taken")
        self.eid_ready = sem("eid_ready")

    def sp(self, sp):
        s = self.slot_of(0)
        parts = [(self.k.slot(s, 0, KC, 72)[:, :, 0:8], rows_of(self.k.arg["w_group_router_3"][0], 0, 8)),
                          (self.k.slot(s, 0, KC, 72)[:, :, 8:72], rows_of(self.k.arg["w_expert_router_3"][0], 0, 64))]
        sp.wait_ge(self.k.w_used, self.freed(0))
        for dst, src in parts:
            sp.dma_start(dst, src).then_inc(self.loaded(0), UNIT_INC // len(parts))

    def pe(self, pe):
        k, nc = self.k, self.k.nc
        pe.wait_ge(self.loaded(0), self.loads(0))
        w = k.slot(self.slot_of(0), 0, KC, 72)
        for t in range(T):
            for c in range(KC):
                last = nc.tensor.matmul(k.bank[:, 0, t * 72:(t + 1) * 72], k.hT[:, c, t * P:(t + 1) * P], w[:, c, :],
                                        start=c == 0, stop=c == KC - 1)
        last.then_inc(k.w_used, 1)
        pe.wait_ge(self.oh_ready, 1)
        nc.tensor.matmul(k.bank[:, 1, 0:128], k.c("lt"), k.oh[:, 2, :, :], start=True, stop=False, skip_group_check=True)
        nc.tensor.matmul(k.bank[:, 1, 64:128], k.c("ones"), k.oh[:, 2, 0, :], start=False, stop=True, skip_group_check=True)
        for t in range(T):
            last = nc.tensor.matmul(k.bank[:, 2, 0:64], k.c("ones"), k.oh[:, 2, t, :], start=t == 0, stop=t == 1)
        last.then_inc(self.rank_ready, 1)
        pe.wait_ge(self.dest_ready, 1)
        for b, src in ((3, k.dest), (4, k.wgt)):
            for n in range(4):
                last = nc.tensor.matmul(k.bank[:, b, n * P:(n + 1) * P], src[:, n:n + 1].to_broadcast([P, P]), k.c("ident"),
                                        start=True, stop=True)
        nc.tensor.transpose(k.bank[0:1, 5, 0:P], k.small[:, 0:1], k.c("ident")).then_inc(self.row_ready, 1)

    def act(self, act, chain):
        k, nc = self.k, self.k.nc
        act.wait_ge(self.exp_in, 1)
        chain(nc.scalar.activation(k.wk[:, 300:316], k.wk[:, 300:316], ACT.Exp))
        chain(nc.scalar.activation(k.small[:, 20:22], k.small[:, 20:22], ACT.Exp), self.exp_out)
        act.wait_ge(self.row_ready, 1)
        chain(nc.scalar.activation(k.drow[:, :], k.bank[:, 3, :], ACT.Copy), self.rows_taken)
        chain(nc.scalar.activation(k.wrow[:, :], k.bank[:, 4, :], ACT.Copy), self.rows_taken)

    def dve(self, dve, chain):
        k, nc = self.k, self.k.nc
        v = nc.vector
        sm, wk = k.small, k.wk

        def tt(out, a, b, op, done=None):
            chain(v.tensor_tensor(out, a, b, op), done)

        def cols(a, n):
            return sm[:, a:a + n]

        def bc(ap, n):
            return ap.rearrange("p (t n) -> p t n", n=1).to_broadcast([P, T, n])

        def iota(n):
            return k.c("iota")[:, 0:n].rearrange("p (t n) -> p t n", t=1).to_broadcast([P, T, n])

        def first_max(src, n, mx, oh, scr):
            chain(v.tensor_reduce(mx, src, AX, ALU.max))
            tt(scr, src, bc(mx, n), ALU.is_equal)
            chain(v.scalar_tensor_tensor(scr, scr, -256.0, iota(n), ALU.mult, ALU.add))
            chain(v.tensor_reduce(cols(30, 2), scr, AX, ALU.min))
            tt(oh, scr, bc(cols(30, 2), n), ALU.is_equal)

        dve.wait_ge(self.k.w_used, self.used(0))
        logits = wk[:, 0:144].rearrange("p (t n) -> p t n", t=T)
        bg = k.r("b_group_router_3").rearrange("p (t n) -> p t n", t=1).to_broadcast([P, T, 8])
        be = k.r("b_expert_router_3").rearrange("p (t n) -> p t n", t=1).to_broadcast([P, T, 64])
        psum = k.bank[:, 0, 0:144].rearrange("p (t n) -> p t n", t=T)
        gl, el = logits[:, :, 0:8], logits[:, :, 8:72]
        tt(gl, psum[:, :, 0:8], bg, ALU.add)
        tt(el, psum[:, :, 8:72], be, ALU.add)
        gsel = wk[:, 160:176].rearrange("p (t n) -> p t n", t=T)
        gscr = wk[:, 176:192].rearrange("p (t n) -> p t n", t=T)
        first_max(gl, 8, cols(4, 2), gsel, gscr)
        ge = wk[:, 300:316].rearrange("p (t n) -> p t n", t=T)
        tt(ge, gl, bc(cols(4, 2), 8), ALU.subtract)
        chain(v.tensor_scalar(gscr, gsel, -1.0, 1e30, ALU.add, ALU.mult))
        for t in range(T):
            e4 = el[:, t, :].rearrange("p (g e) -> p g e", g=8)
            tt(e4, e4, gscr[:, t, :].rearrange("p (g e) -> p g e", e=1).to_broadcast([P, 8, 8]), ALU.add)
        scr = wk[:, 400:528].rearrange("p (t n) -> p t n", t=T)
        first_max(el, 64, cols(6, 2), k.oh[:, 0, :, :], scr)
        chain(v.scalar_tensor_tensor(el, k.oh[:, 0, :, :], -3e30, el, ALU.mult, ALU.add))
        first_max(el, 64, cols(8, 2), k.oh[:, 1, :, :], scr)
        tt(k.oh[:, 2, :, :], k.oh[:, 0, :, :], k.oh[:, 1, :, :], ALU.add, self.oh_ready)
        tt(cols(20, 2), cols(8, 2), cols(6, 2), ALU.subtract, self.exp_in)
        dve.wait_ge(self.exp_out, 1)
        chain(v.tensor_reduce(cols(10, 2), ge, AX, ALU.add))
        chain(v.tensor_scalar(cols(12, 2), cols(20, 2), 1.0, None, ALU.add))
        tt(cols(12, 2), cols(12, 2), cols(10, 2), ALU.mult)
        chain(v.reciprocal(k.wgt[:, 0:2], cols(12, 2)))
        tt(k.wgt[:, 2:4], k.wgt[:, 0:2], cols(20, 2), ALU.mult)
        dve.wait_ge(self.rank_ready, 1)
        cnt = k.bank[:, 2, 0:64]
        nb, end, big = wk[:, 600:664], wk[:, 664:728], wk[:, 728:792]
        chain(v.tensor_scalar(nb, cnt, 0.5, None, ALU.is_gt))
        chain(v.scalar_tensor_tensor(nb, cnt, SLOTS + 0.5, nb, ALU.is_gt, ALU.add))
        chain(v.memset(big, 0.0))
        chain(v.tensor_tensor_scan(end, nb, big, 0.0, ALU.add, ALU.add))
        tt(nb, end, nb, ALU.subtract)
        slots = wk[:, 800:928].rearrange("p (t n) -> p t n", t=T)
        chain(v.scalar_tensor_tensor(slots, nb.rearrange("p (t n) -> p t n", t=1).to_broadcast([P, T, 64]), float(SLOTS),
                                     k.bank[:, 1, 0:128].rearrange("p (t n) -> p t n", t=T), ALU.mult, ALU.add))
        for c in range(2):
            tt(scr, slots, k.oh[:, c, :, :], ALU.mult)
            chain(v.tensor_reduce(k.dest[:, 2 * c:2 * c + 2], scr, AX, ALU.add))
        chain(v.tensor_scalar(wk[:, 728:792], end, k.c("row"), None, ALU.is_le))
        chain(v.tensor_reduce(cols(1, 1), wk[:, 728:792], AX, ALU.add))
        chain(v.tensor_scalar(cols(0, 1), cols(1, 1), float(NEXP - 1), None, ALU.min), self.dest_ready)
        dve.wait_ge(self.row_ready, 1)
        chain(v.tensor_copy(k.eid[0:1, :], k.bank[0:1, 5, 0:P]), self.eid_ready)
        chain(v.tensor_copy(k.pslot[:, 0:1], k.c("row")))


class Experts(Stage):
    UNITS = NBLK * 3
    BODY = NSLOT * 3
    G, XG, SI, HI, HT, Y, GW, TM = 0, 512, 1536, 2048, 2560, 3072, 4096, 4608
    PUT_BANKS = (0, 1, 4, 7)

    def name_sems(self, sem):
        self.sel_ready = sem("sel_ready")
        self.xg_ready = sem("xg_ready")
        self.xg_taken = sem("xg_taken")
        self.silu_ready = sem("silu_ready")
        self.hid_ready = sem("hid_ready")
        self.ht_ready = sem("ht_ready")
        self.ht_taken = sem("ht_taken")
        self.y_taken = sem("y_taken")
        self.put_ready = sem("put_ready")
        self.put_taken = sem("put_taken")
        self.gw_ready = sem("gw_ready")

    def __init__(self, k, name, route):
        super().__init__(k, name)
        self.route = route

    def w(self, base, n):
        return self.k.wk[:, base:base + n]

    def sp(self, sp):
        k = self.k
        sp.wait_ge(self.route.eid_ready, 1)
        with sp.Fori(0, NBLK // NSLOT) as i:
            for s in range(NSLOT):
                e = sp.value_load(k.eid[0:1, bass.ds(i * NSLOT + s, 1)], min_val=0, max_val=NEXP - 1)
                for n, name in enumerate(("w_expert_gate_3", "w_expert_up_3", "w_expert_down_3")):
                    j = s * 3 + n
                    slot = self.slot_of(j)
                    w = k.arg[name][0][bass.ds(e, 1), :, :].rearrange("e (a p) n -> p (e a) n", p=P)
                    sp.wait_ge(k.w_used, i * self.BODY + (self.u0 + j + 1))
                    sp.dma_start(k.slot(slot, 0, 8, 512) if n < 2 else k.slot(slot, 0, 4, DM), w).then_inc(self.loaded(j), UNIT_INC)

    def pe(self, pe):
        k, nc = self.k, self.k.nc

        def gather():
            g = self.w(self.G, 256)
            for c in range(KC):
                for t in range(T):
                    last = nc.tensor.matmul(k.bank[:, c // 4, (c % 4) * P:(c % 4 + 1) * P], k.xn[:, t, c * P:(c + 1) * P],
                                            g[:, t * P:(t + 1) * P], start=t == 0, stop=t == 1)
            last.then_inc(self.xg_ready, 1)

        def put(parity):
            gw, y = self.w(self.GW + parity * S, S), self.w(self.Y, DM)
            for n, bank in enumerate(self.PUT_BANKS):
                nc.tensor.matmul(k.bank[:, bank, :], gw[:, (n // 2) * P:(n // 2 + 1) * P], y[:, (n % 2) * 512:(n % 2 + 1) * 512],
                                 start=True, stop=True).then_inc(self.put_ready, 1)

        def block(b, s, i):
            xg, ht = self.w(self.XG, DM), self.w(self.HT, 512)
            pe.wait_ge(self.xg_taken, b + 1)
            for n in range(2):
                pe.wait_ge(self.loaded(3 * s + n), self.loads(3 * s + n, i * 3))
                w = k.slot(self.slot_of(3 * s + n), 0, KC, 512)
                for c in range(KC):
                    last = nc.tensor.matmul(k.bank[:, 2 + n, :], xg[:, c * P:(c + 1) * P], w[:, c, :],
                                            start=c == 0, stop=c == KC - 1)
                last.then_inc(k.w_used, 1)
            pe.wait_ge(self.y_taken, b + 1)
            pe.wait_ge(self.gw_ready, b + 1)
            pe.wait_ge(self.put_taken, b * 4 + 4)
            put((s + 1) % 2)
            pe.wait_ge(self.hid_ready, b + 1)
            for c in range(4):
                last = nc.tensor.transpose(k.bank[:, 2, c * P:(c + 1) * P], self.w(self.HI + c * P, P), k.c("ident"))
            last.then_inc(self.ht_ready, 1)
            pe.wait_ge(self.sel_ready, b + 2)
            pe.wait_ge(self.put_taken, b * 4 + 6)
            gather()
            pe.wait_ge(self.ht_taken, b + 1)
            pe.wait_ge(self.loaded(3 * s + 2), self.loads(3 * s + 2, i * 3))
            w = k.slot(self.slot_of(3 * s + 2), 0, 4, DM)
            for h in range(2):
                for c in range(4):
                    last = nc.tensor.matmul(k.bank[:, 5 + h, :], ht[:, c * P:(c + 1) * P], w[:, c, h * 512:(h + 1) * 512],
                                            start=c == 0, stop=c == 3)
            last.then_inc(k.w_used, 1)

        pe.sem_inc(self.put_taken, 4)
        pe.wait_ge(self.sel_ready, 1)
        gather()
        with pe.Fori(0, NBLK // NSLOT) as i:
            for s in range(NSLOT):
                block(i * NSLOT + s, s, i)
        pe.wait_ge(self.y_taken, NBLK + 1)
        pe.wait_ge(self.gw_ready, NBLK + 1)
        pe.wait_ge(self.put_taken, 4 * NBLK + 4)
        pe.wait_ge(self.xg_taken, NBLK + 1)
        put(1)

    def act(self, act, chain):
        k, nc = self.k, self.k.nc
        with act.Fori(0, NBLK // NSLOT) as i:
            for s in range(NSLOT):
                b = i * NSLOT + s
                act.wait_ge(self.k.w_used, self.used(b * 3 + 1))
                nc.scalar.activation(self.w(self.SI, 512), k.bank[:, 2, :], ACT.Silu).then_inc(self.silu_ready, 1)
                act.wait_ge(self.ht_ready, b + 1)
                nc.scalar.activation(self.w(self.HT, 512), k.bank[:, 2, :], ACT.Copy).then_inc(self.ht_taken, 1)
                act.wait_ge(self.k.w_used, self.used(b * 3 + 2))
                nc.scalar.activation(self.w(self.Y, DM).rearrange("p (a n) -> p a n", a=2), k.bank[:, 5:7, :],
                                     ACT.Copy).then_inc(self.y_taken, 1)

    def dve(self, dve, chain):
        k, nc = self.k, self.k.nc
        v = nc.vector
        slots, part = k.pslot[:, 0:4], k.pslot[:, 4:5]

        def select():
            for t in range(T):
                g = self.w(self.G + t * P, P)
                chain(v.tensor_scalar(g, k.c("iota"), slots[:, t:t + 1], None, ALU.is_equal))
                chain(v.scalar_tensor_tensor(g, k.c("iota"), slots[:, 2 + t:3 + t], g, ALU.is_equal, ALU.add),
                      self.sel_ready if t else None)
            chain(v.tensor_scalar(slots, slots, float(SLOTS), None, ALU.subtract))

        def scatter_matrix(parity):
            gw, tm = self.w(self.GW + parity * S, S), self.w(self.TM, S)
            chain(v.scalar_tensor_tensor(gw, k.drow[:, 0:S], part, k.wrow[:, 0:S], ALU.is_equal, ALU.mult))
            chain(v.scalar_tensor_tensor(tm, k.drow[:, S:2 * S], part, k.wrow[:, S:2 * S], ALU.is_equal, ALU.mult))
            chain(v.tensor_tensor(gw, gw, tm, ALU.add), self.gw_ready)
            chain(v.tensor_scalar(part, part, float(SLOTS), None, ALU.add))

        def take_tokens():
            for b in range(2):
                g = k.p("norm_ffn_w_3", 4 * b, 4).rearrange("p (a n) -> p a n", n=1).to_broadcast([P, 4, SLOTS])
                last = v.tensor_tensor(self.w(self.XG + 512 * b, 512).rearrange("p (a n) -> p a n", a=4),
                                       k.bank[:, b, :].rearrange("p (a n) -> p a n", a=4), g, ALU.mult)
                chain(last, self.xg_taken if b else None)

        def take_put():
            for n, bank in enumerate(self.PUT_BANKS):
                x = k.x[:, n // 2, (n % 2) * 512:(n % 2 + 1) * 512]
                chain(v.tensor_tensor(x, k.bank[:, bank, :], x, ALU.add), self.put_taken)

        chain.credit(self.put_taken, 4)
        chain(v.memset(self.w(self.Y, DM), 0.0), self.y_taken)
        chain(v.memset(self.w(self.GW + S, S), 0.0), self.gw_ready)
        chain(v.tensor_copy(slots, k.dest[:, :]))
        chain(v.tensor_copy(part, k.c("row")))
        select()
        dve.wait_ge(self.xg_ready, 1)
        take_tokens()
        with dve.Fori(0, NBLK // NSLOT) as i:
            chain.enter(i, NSLOT * 8, [(self.sel_ready, NSLOT), (self.gw_ready, NSLOT), (self.hid_ready, NSLOT),
                                       (self.put_taken, NSLOT * 4), (self.xg_taken, NSLOT)])
            for s in range(NSLOT):
                b = i * NSLOT + s
                select()
                scatter_matrix(s % 2)
                dve.wait_ge(self.silu_ready, b + 1)
                chain(v.tensor_tensor(self.w(self.HI, 512), k.bank[:, 3, :], self.w(self.SI, 512), ALU.mult), self.hid_ready)
                dve.wait_ge(self.put_ready, b * 4 + 4)
                take_put()
                dve.wait_ge(self.xg_ready, b + 2)
                take_tokens()
        chain.leave(NBLK // NSLOT)
        dve.wait_ge(self.put_ready, 4 * NBLK + 4)
        take_put()


class Store(Stage):

    def name_sems(self, sem):
        self.stored = sem("stored")

    def act(self, act, chain):
        k = self.k
        act.dma_start(k.arg["out"].rearrange("a (t p) n -> p (a t) n", p=P), k.x[:, :, :]).then_inc(self.stored, 16)
        act.wait_ge(self.stored, 16)


def first_block(k):
    a, big, plan = k.arg, k.big, []
    for i in range(2):
        plan += [Norm(k, f"n{i}a", ("norm_g", (3 * i) * KC)), GatedUp(k, f"up{i}a", a["ffn_w_in"][i, 0]),
                 Project(k, f"dn{i}a", big, FC, a["ffn_w_out"][i, 0], 0.5),
                 Norm(k, f"n{i}b", ("norm_g", (3 * i + 1) * KC))]
        if i == 0:
            plan += [ConvGlu(k, "glu"), DepthConv(k, "dwc"),
                     Project(k, "pw2", big, KC, a["conv_w_pw2"][0], 1.0, "conv_b_pw2")]
        else:
            plan += [Stick(k, "stick", a["attn_w_qkv"][0], 0, DM, 2 * DM), Project(k, "swo", big, KC, a["attn_w_o"][0])]
        plan += [Norm(k, f"n{i}c", ("norm_g", (3 * i + 2) * KC)), GatedUp(k, f"up{i}c", a["ffn_w_in"][i, 1]),
                 Project(k, f"dn{i}c", big, FC, a["ffn_w_out"][i, 1], 0.5)]
    return plan + [FinalNorm(k, "f1", "final_g")]


def merged(k):
    return k.wk[:, 0:KC * S].rearrange("p (c n) -> p c n", c=KC)


def second_block(k):
    a, big, mt = k.arg, k.big, merged(k)
    w_in = a["w_in_2"][0]
    return [Norm(k, "n2a", ("attn_norm_2", 0)), Latent(k, "lat"), Mla(k, "mla"),
             Roped(k, "moba", w_in, 704, 1728, 2752, 1, 128.0 ** -0.5, "rot128", "cos128", "sin128", 8),
             Merge(k, "mrg2", big[:, 0:8, :], a["w_o_mla_2"][0], big[:, 8:16, :], a["w_o_moba_2"][0], w_in, 3776, 4800, "b_gate_2"),
             Project(k, "out2", mt, KC, a["w_out_2"][0]),
             Norm(k, "n2b", ("ffn_norm_2", 0)), ConvUp(k, "cup", a["w_up_2"][0]), Project(k, "dn2", big, FC, a["w_down_2"][0]),
             FinalNorm(k, "f2", "final_norm_2")]


def third_block(k):
    a, big, mt = k.arg, k.big, merged(k)
    w_in = a["w_in_3"][0]
    cos, sin = k.wk[:, 8192:8192 + S], k.wk[:, 8192 + S:8192 + 2 * S]
    plan = [Norm(k, "n3a", ("norm_mix_w_3", 0)), Angles(k, "ang"),
             Roped(k, "diff", w_in, 0, DM, 2 * DM, 2, 0.125, "rot64", cos, sin, 16), SubNorm(k, "sub"),
             StepSizes(k, "dt"), Ssd(k, "ssd"),
             Merge(k, "mrg3", big[:, 16:24, :], a["w_branch_attn_3"][0], big[:, 0:16, :], a["w_branch_ssd_3"][0], w_in, 9248, 10272, None),
             Project(k, "out3", mt, KC, a["w_out_3"][0]),
             Norm(k, "n3b", ("norm_ffn_w_3", 0))]
    route = Route(k, "route")
    plan += [route, Experts(k, "moe", route), FinalNorm(k, "f3", "final_norm_w_3")]
    return plan


def stages(k):
    return [Setup(k, "setup")] + first_block(k) + second_block(k) + third_block(k) + [Store(k, "store")]


def build(nc, arg, only=None):
    with ExitStack() as ctx:
        k = Core(nc, ctx, arg)
        k.pos = k.sb("pos", [P, S], I32)
        k.sd = k.sb("sd", [P, 8, 32])
        k.oh = k.sb("oh", [P, 3, T, NEXP])
        k.dest, k.wgt = k.sb("dest", [P, 4]), k.sb("wgt", [P, 4])
        k.drow, k.wrow = k.sb("drow", [P, 2 * S]), k.sb("wrow", [P, 2 * S])
        k.eid = k.sb("eid", [P, P], I32)
        k.small, k.pslot = k.sb("small", [P, 40]), k.sb("pslot", [P, 8])
        plan = (only or stages)(k)
        block = ctx.enter_context(nc.Block())

        def run(eng, kind, chain=None):
            for n, stage in enumerate(plan):
                f = {"pe": stage.pe, "act": stage.act, "dve": stage.dve, "pool": stage.pool}[kind]
                f(eng, chain) if chain is not None else f(eng)
                eng.drain().then_inc(k.barrier, 1)
                eng.wait_ge(k.barrier, LANES * (n + 1))

        @block.sync
        def _(sp):
            for stage in plan:
                stage.sp(sp)

        @block.tensor
        def _(pe):
            pe.sem_inc(k.w_used, NSLOT)
            run(pe, "pe")

        @block.scalar
        def _(act):
            run(act, "act", Chain(act, k.chain_sem["act"]))

        @block.vector
        def _(dve):
            run(dve, "dve", Chain(dve, k.chain_sem["dve"]))

        @block.gpsimd
        def _(pool):
            run(pool, "pool", Chain(pool, k.chain_sem["pool"]))


def lay_out(inputs):
    arrays = {"x": np.asarray(inputs["x"]), "positions_3": np.asarray(inputs["positions_3"]), "constants": CONST_ARRAY}
    arrays["params"] = np.ascontiguousarray(
        np.concatenate([np.asarray(inputs[n]).reshape(-1, P) for n in PARAM_NAMES], 0).T)
    arrays["rows"] = np.concatenate([np.asarray(inputs[n]).reshape(1, -1) for n in ROW_NAMES], 1)
    for n in WEIGHTS:
        arrays[n] = np.asarray(inputs[n])
    return arrays


def kernel(**inputs):
    import concourse.bacc as bacc
    from concourse.bass_utils import run_bass_kernel_spmd

    nc = bacc.Bacc("TRN2", target_bir_lowering=False, num_devices=1)
    arrays = lay_out(inputs)
    arg = {n: nc.dram_tensor("in_" + n, a.shape, mybir.dt.from_np(a.dtype), kind="ExternalInput").ap()
           for n, a in arrays.items()}
    arg["out"] = nc.dram_tensor("out", (1, S, DM), F32, kind="ExternalOutput").ap()
    build(nc, arg)
    r = run_bass_kernel_spmd(nc, [{"in_" + n: a for n, a in arrays.items()}], core_ids=[0])
    return r.results[0]["out"]
```
